# Optimizing a Trainium2 kernel written in Bass

```python
import jax, jax.numpy as jnp
from jax import lax
import numpy as np

D_MODEL = 1024
BATCH = 1
SEQ = 256
DEPTH = 2

GRID_W = 64
CTX_LEN = 256
HEAD_DIM = 64
ATTN_W = D_MODEL // 2
N_Q_HEADS = ATTN_W // HEAD_DIM
N_KV_HEADS = N_Q_HEADS // 4
Q_PER_KV = N_Q_HEADS // N_KV_HEADS
KV_W = N_KV_HEADS * HEAD_DIM
POOL_W = D_MODEL // 4
POOL_WINDOWS = (2, 4, 8, 16)
N_POOL_GROUPS = len(POOL_WINDOWS)
POOL_GROUP_W = POOL_W // N_POOL_GROUPS
FFT_W = D_MODEL // 4
N_FFT_GROUPS = 4
FFT_GROUP_W = FFT_W // N_FFT_GROUPS
MIX_W = ATTN_W + POOL_W + FFT_W
IN_W = ATTN_W + 2 * KV_W + POOL_W + FFT_W
D_FF = ((8 * D_MODEL // 3 + 127) // 128) * 128
ROPE_THETA = 10000.0
Q_BLOCK = 128
N_MOD = 9
EPS = 1e-6
ATTN_SCALE = HEAD_DIM ** -0.5


def rms_norm(x):
    xf = x.astype(jnp.float32)
    return (xf * lax.rsqrt(jnp.mean(xf * xf, axis=-1, keepdims=True) + EPS)).astype(x.dtype)

def modulate(h, shift, scale):
    return h * (1 + scale[:, None, :]) + shift[:, None, :]

def swiglu(h, w_gu, w_down):
    g, u = jnp.split(h @ w_gu, 2, axis=-1)
    return (jax.nn.silu(g) * u) @ w_down

def axial_rope_tables(length):
    rows = length // GRID_W
    row = jnp.repeat(jnp.arange(rows), GRID_W).astype(jnp.float32)
    col = jnp.tile(jnp.arange(GRID_W), rows).astype(jnp.float32)
    n_freq = HEAD_DIM // 4
    inv_freq = ROPE_THETA ** (-jnp.arange(n_freq, dtype=jnp.float32) / n_freq)
    ang = jnp.concatenate([row[:, None] * inv_freq, col[:, None] * inv_freq], axis=-1)
    return jnp.cos(ang), jnp.sin(ang)

def apply_rope(x, cos, sin):
    shape = (1, cos.shape[0]) + (1,) * (x.ndim - 3) + (cos.shape[1],)
    cos = cos.reshape(shape).astype(x.dtype)
    sin = sin.reshape(shape).astype(x.dtype)
    half = HEAD_DIM // 2
    x1, x2 = x[..., :half], x[..., half:]
    return jnp.concatenate([x1 * cos - x2 * sin, x1 * sin + x2 * cos], axis=-1)

def split_in(z):
    b = [ATTN_W, ATTN_W + KV_W, ATTN_W + 2 * KV_W, ATTN_W + 2 * KV_W + POOL_W]
    return jnp.split(z, b, axis=-1)

def q_heads(q, gain):
    q = q.reshape(q.shape[:2] + (N_KV_HEADS, Q_PER_KV, HEAD_DIM))
    return rms_norm(q) * gain

def kv_heads(t):
    return t.reshape(t.shape[:2] + (N_KV_HEADS, HEAD_DIM))

def attend_latent(q, k, v, k_ctx, v_ctx):
    k_all = jnp.concatenate([k, k_ctx], axis=1)
    v_all = jnp.concatenate([v, v_ctx], axis=1)
    bsz, length = q.shape[:2]
    n_blk = length // Q_BLOCK
    qb = q.reshape((bsz, n_blk, Q_BLOCK) + q.shape[2:]).transpose(1, 0, 2, 3, 4, 5)

    def one_block(q_blk):
        s = jnp.einsum('bqkgd,bskd->bkgqs', q_blk, k_all).astype(jnp.float32) * ATTN_SCALE
        p = jax.nn.softmax(s, axis=-1).astype(v_all.dtype)
        return jnp.einsum('bkgqs,bskd->bqkgd', p, v_all)

    o = lax.map(one_block, qb)
    return o.transpose(1, 0, 2, 3, 4, 5).reshape(bsz, length, ATTN_W)

def attend_context(q, k, v):
    s = jnp.einsum('bqkgd,bskd->bkgqs', q, k).astype(jnp.float32) * ATTN_SCALE
    p = jax.nn.softmax(s, axis=-1).astype(v.dtype)
    o = jnp.einsum('bkgqs,bskd->bqkgd', p, v)
    return o.reshape(q.shape[0], q.shape[1], ATTN_W)

def pool_minus_self(u):
    bsz, length, _ = u.shape
    ug = u.reshape(bsz, length, N_POOL_GROUPS, POOL_GROUP_W).astype(jnp.float32)
    cs = jnp.cumsum(ug, axis=1)
    cs = jnp.concatenate([jnp.zeros_like(cs[:, :1]), cs], axis=1)
    t = jnp.arange(length)
    means = []
    for g, w in enumerate(POOL_WINDOWS):
        lo = jnp.clip(t - w // 2, 0, length)
        hi = jnp.clip(t + w - w // 2, 0, length)
        cs_g = cs[:, :, g]
        s = jnp.take(cs_g, hi, axis=1) - jnp.take(cs_g, lo, axis=1)
        cnt = (hi - lo).astype(jnp.float32)[None, :, None]
        means.append(s / cnt)
    mean = jnp.stack(means, axis=2)
    return (mean - ug).astype(u.dtype)

def fourier_2d(u):
    bsz, length, _ = u.shape
    ug = u.reshape(bsz, length, N_FFT_GROUPS, FFT_GROUP_W).astype(jnp.float32)
    f = jnp.fft.fft2(ug, axes=(1, 3), norm='ortho').real
    return f.reshape(bsz, length, FFT_W).astype(u.dtype)

def merge_mixers(attn_out, u_pool, u_fft, pool_w_l, pool_scale_l, fft_w_l, w_out_l):
    bsz, length, _ = u_pool.shape
    yp = jnp.einsum('blgc,gcd->blgd', pool_minus_self(u_pool), pool_w_l).reshape(bsz, length, POOL_W) * pool_scale_l
    yf = fourier_2d(u_fft) @ fft_w_l
    return jnp.concatenate([attn_out, yp, yf], axis=-1) @ w_out_l

def first_inputs(seed: int = 0) -> dict:
    key = jax.random.key(seed)
    ks = jax.random.split(key, 20)

    def nrm(k, shape, std):
        return jax.random.normal(k, shape, jnp.float32) * std

    return {
        'x': nrm(ks[0], (BATCH, SEQ, D_MODEL), 1.0),
        'c': nrm(ks[1], (BATCH, D_MODEL), 1.0),
        'ctx': nrm(ks[2], (BATCH, CTX_LEN, D_MODEL), 1.0),
        'c_ctx': nrm(ks[3], (D_MODEL,), 1.0),
        'ada_w': nrm(ks[4], (DEPTH, D_MODEL, N_MOD * D_MODEL), 0.5 * D_MODEL ** -0.5),
        'ada_b': nrm(ks[5], (DEPTH, N_MOD * D_MODEL), 0.01),
        'ffn1_w_gu': nrm(ks[6], (DEPTH, D_MODEL, 2 * D_FF), D_MODEL ** -0.5),
        'ffn1_w_down': nrm(ks[7], (DEPTH, D_FF, D_MODEL), D_FF ** -0.5),
        'w_in': nrm(ks[8], (DEPTH, D_MODEL, IN_W), D_MODEL ** -0.5),
        'q_gain': 1.0 + nrm(ks[9], (DEPTH, HEAD_DIM), 0.1),
        'k_gain': 1.0 + nrm(ks[10], (DEPTH, HEAD_DIM), 0.1),
        'pool_w': nrm(ks[11], (DEPTH, N_POOL_GROUPS, POOL_GROUP_W, POOL_GROUP_W), POOL_GROUP_W ** -0.5),
        'pool_scale': 1.0 + nrm(ks[12], (DEPTH, POOL_W), 0.1),
        'fft_w': nrm(ks[13], (DEPTH, FFT_W, FFT_W), FFT_W ** -0.5),
        'w_out': nrm(ks[14], (DEPTH, MIX_W, D_MODEL), MIX_W ** -0.5),
        'ffn2_w_gu': nrm(ks[15], (DEPTH, D_MODEL, 2 * D_FF), D_MODEL ** -0.5),
        'ffn2_w_down': nrm(ks[16], (DEPTH, D_FF, D_MODEL), D_FF ** -0.5),
        'final_gain': 1.0 + nrm(ks[17], (D_MODEL,), 0.1),
    }

def first_block(x, c, ctx, c_ctx, ada_w, ada_b, ffn1_w_gu, ffn1_w_down, w_in, q_gain, k_gain,
              pool_w, pool_scale, fft_w, w_out, ffn2_w_gu, ffn2_w_down, final_gain):
    cos, sin = axial_rope_tables(x.shape[1])
    for layer in range(DEPTH):
        last = layer == DEPTH - 1
        mx = jnp.split(jax.nn.silu(c) @ ada_w[layer] + ada_b[layer], N_MOD, axis=-1)
        mc = jnp.split((jax.nn.silu(c_ctx) @ ada_w[layer] + ada_b[layer])[None, :], N_MOD, axis=-1)

        x = x + 0.5 * mx[2][:, None] * swiglu(modulate(rms_norm(x), mx[0], mx[1]), ffn1_w_gu[layer], ffn1_w_down[layer])
        ctx = ctx + 0.5 * mc[2][:, None] * swiglu(modulate(rms_norm(ctx), mc[0], mc[1]), ffn1_w_gu[layer], ffn1_w_down[layer])

        hx = modulate(rms_norm(x), mx[3], mx[4])
        hc = modulate(rms_norm(ctx), mc[3], mc[4])
        if last:
            kc, vc = jnp.split(hc @ w_in[layer, :, ATTN_W:ATTN_W + 2 * KV_W], 2, axis=-1)
        else:
            qc, kc, vc, upc, ufc = split_in(hc @ w_in[layer])
        kc = rms_norm(kv_heads(kc)) * k_gain[layer]
        vc = kv_heads(vc)

        qx, kx, vx, upx, ufx = split_in(hx @ w_in[layer])
        qx = apply_rope(q_heads(qx, q_gain[layer]), cos, sin)
        kx = apply_rope(rms_norm(kv_heads(kx)) * k_gain[layer], cos, sin)
        vx = kv_heads(vx)
        ax = attend_latent(qx, kx, vx, kc, vc)
        x = x + mx[5][:, None] * merge_mixers(ax, upx, ufx, pool_w[layer], pool_scale[layer], fft_w[layer], w_out[layer])

        x = x + 0.5 * mx[8][:, None] * swiglu(modulate(rms_norm(x), mx[6], mx[7]), ffn2_w_gu[layer], ffn2_w_down[layer])

        if not last:
            ac = attend_context(q_heads(qc, q_gain[layer]), kc, vc)
            ctx = ctx + mc[5][:, None] * merge_mixers(ac, upc, ufc, pool_w[layer], pool_scale[layer], fft_w[layer], w_out[layer])
            ctx = ctx + 0.5 * mc[8][:, None] * swiglu(modulate(rms_norm(ctx), mc[6], mc[7]), ffn2_w_gu[layer], ffn2_w_down[layer])

    return rms_norm(x) * final_gain


DEPTH_2 = 4

N_MIXERS = 3
N_A = (DEPTH_2 + 2) // 3
N_B = (DEPTH_2 + 1) // 3
N_C = DEPTH_2 // 3
D_RNN = 1280
A_HEADS = 16
A_HEAD_DIM = D_RNN // A_HEADS
A_CONV = 4
LRU_C = 8.0
D_SGU = D_MODEL
SGU_CHUNK = 128
SGU_GROUPS = 8
SGU_GROUP_DIM = D_SGU // SGU_GROUPS
D_CONV = D_MODEL
C_CONV = 3
D_FF_2 = 4 * D_MODEL


def _rmsnorm(x, g):
    x32 = x.astype(jnp.float32)
    y = x32 * lax.rsqrt(jnp.mean(x32 * x32, axis=-1, keepdims=True) + EPS)
    return y.astype(x.dtype) * g

def _causal_dwconv(x, w):
    k = w.shape[0]
    return lax.conv_general_dilated(
        x, w[:, None, :].astype(x.dtype), window_strides=(1,),
        padding=[(k - 1, 0)], dimension_numbers=("NWC", "WIO", "NWC"),
        feature_group_count=x.shape[-1])

def _lru_combine(left, right):
    a_l, b_l = left
    a_r, b_r = right
    return a_l * a_r, a_r * b_l + b_r

def _rglru_mixer(h, w_in, conv_w, conv_b, gate_a_w, gate_a_b, gate_x_w, gate_x_b, lam, w_out):
    b, s, _ = h.shape
    gate, xr = jnp.split(h @ w_in, 2, axis=-1)
    gate = jax.nn.gelu(gate)
    xr = _causal_dwconv(xr, conv_w) + conv_b
    xh = xr.reshape(b, s, A_HEADS, A_HEAD_DIM)
    r = jax.nn.sigmoid(jnp.einsum("bshi,hij->bshj", xh, gate_a_w).reshape(b, s, D_RNN) + gate_a_b)
    ig = jax.nn.sigmoid(jnp.einsum("bshi,hij->bshj", xh, gate_x_w).reshape(b, s, D_RNN) + gate_x_b)
    log_a = -LRU_C * r.astype(jnp.float32) * jax.nn.softplus(-lam.astype(jnp.float32))
    a = jnp.exp(log_a)
    u = jnp.sqrt(-jnp.expm1(2.0 * log_a)) * (ig * xr).astype(jnp.float32)
    _, hs = lax.associative_scan(_lru_combine, (a, u), axis=1)
    return (hs.astype(h.dtype) * gate) @ w_out

def _sgu_mixer(h, w_in, norm_g, w_s, s_bias, w_out):
    b, s, _ = h.shape
    z = jax.nn.gelu(h @ w_in)
    u, v = jnp.split(z, 2, axis=-1)
    v = _rmsnorm(v, norm_g)
    n_chunks = s // SGU_CHUNK
    v = v.reshape(b, n_chunks, SGU_CHUNK, SGU_GROUPS, SGU_GROUP_DIM)
    causal = jnp.tril(jnp.ones((SGU_CHUNK, SGU_CHUNK), dtype=bool))
    w_causal = jnp.where(causal[None], w_s, jnp.zeros((), w_s.dtype))
    mixed = jnp.einsum("gts,bnsgc->bntgc", w_causal, v) + s_bias.T[None, None, :, :, None]
    y = u * mixed.reshape(b, s, D_SGU)
    return y @ w_out

def _shortconv_mixer(h, w_in, conv_w, w_out):
    gb, gc, xv = jnp.split(h @ w_in, 3, axis=-1)
    y = gb * _causal_dwconv(gc * xv, conv_w)
    return y @ w_out

def _sqrelu_mlp(h, w1, w2):
    return jnp.square(jax.nn.relu(h @ w1)) @ w2

def second_inputs(seed: int = 0) -> dict:
    key = jax.random.key(seed)
    ks = jax.random.split(key, 24)
    f32 = jnp.float32

    def w(k, shape, fan_in):
        return jax.random.normal(k, shape, f32) * (fan_in ** -0.5)

    def gain(k, shape):
        return 1.0 + 0.1 * jax.random.normal(k, shape, f32)

    def bias(k, shape, scale=0.1):
        return scale * jax.random.normal(k, shape, f32)

    a_c = jax.random.uniform(ks[11], (N_A, D_RNN), f32, minval=0.9, maxval=0.999)
    a0 = a_c ** (1.0 / LRU_C)
    a_lambda = jnp.log(a0) - jnp.log1p(-a0)

    return {
        "x": jax.random.normal(ks[0], (BATCH, SEQ, D_MODEL), f32),
        "norm_mix_g": gain(ks[1], (DEPTH_2, D_MODEL)),
        "norm_mlp_g": gain(ks[2], (DEPTH_2, D_MODEL)),
        "final_norm_g": gain(ks[3], (D_MODEL,)),
        "a_w_in": w(ks[4], (N_A, D_MODEL, 2 * D_RNN), D_MODEL),
        "a_conv_w": w(ks[5], (N_A, A_CONV, D_RNN), A_CONV),
        "a_conv_b": bias(ks[6], (N_A, D_RNN)),
        "a_gate_a_w": w(ks[7], (N_A, A_HEADS, A_HEAD_DIM, A_HEAD_DIM), A_HEAD_DIM),
        "a_gate_a_b": bias(ks[8], (N_A, D_RNN)),
        "a_gate_x_w": w(ks[9], (N_A, A_HEADS, A_HEAD_DIM, A_HEAD_DIM), A_HEAD_DIM),
        "a_gate_x_b": bias(ks[10], (N_A, D_RNN)),
        "a_lambda": a_lambda,
        "a_w_out": w(ks[12], (N_A, D_RNN, D_MODEL), D_RNN),
        "b_w_in": w(ks[13], (N_B, D_MODEL, 2 * D_SGU), D_MODEL),
        "b_norm_g": gain(ks[14], (N_B, D_SGU)),
        "b_w_s": w(ks[15], (N_B, SGU_GROUPS, SGU_CHUNK, SGU_CHUNK), SGU_CHUNK),
        "b_s_bias": gain(ks[16], (N_B, SGU_GROUPS, SGU_CHUNK)),
        "b_w_out": w(ks[17], (N_B, D_SGU, D_MODEL), D_SGU),
        "c_w_in": w(ks[18], (N_C, D_MODEL, 3 * D_CONV), D_MODEL),
        "c_conv_w": w(ks[19], (N_C, C_CONV, D_CONV), C_CONV),
        "c_w_out": w(ks[20], (N_C, D_CONV, D_MODEL), D_CONV),
        "mlp_w1": w(ks[21], (DEPTH_2, D_MODEL, D_FF_2), D_MODEL),
        "mlp_w2": w(ks[22], (DEPTH_2, D_FF_2, D_MODEL), D_FF_2),
    }

def second_block(x, norm_mix_g, norm_mlp_g, final_norm_g,
              a_w_in, a_conv_w, a_conv_b, a_gate_a_w, a_gate_a_b, a_gate_x_w, a_gate_x_b, a_lambda, a_w_out,
              b_w_in, b_norm_g, b_w_s, b_s_bias, b_w_out,
              c_w_in, c_conv_w, c_w_out,
              mlp_w1, mlp_w2):
    for i in range(DEPTH_2):
        kind, j = i % N_MIXERS, i // N_MIXERS
        h = _rmsnorm(x, norm_mix_g[i])
        if kind == 0:
            mix = _rglru_mixer(h, a_w_in[j], a_conv_w[j], a_conv_b[j], a_gate_a_w[j], a_gate_a_b[j],
                               a_gate_x_w[j], a_gate_x_b[j], a_lambda[j], a_w_out[j])
        elif kind == 1:
            mix = _sgu_mixer(h, b_w_in[j], b_norm_g[j], b_w_s[j], b_s_bias[j], b_w_out[j])
        else:
            mix = _shortconv_mixer(h, c_w_in[j], c_conv_w[j], c_w_out[j])
        x = x + mix
        x = x + _sqrelu_mlp(_rmsnorm(x, norm_mlp_g[i]), mlp_w1[i], mlp_w2[i])
    return _rmsnorm(x, final_norm_g)


def setup_inputs(seed=0):
    out = dict(first_inputs(seed))
    for name, value in second_inputs(seed + 1).items():
        if name != "x":
            out[name + "_2"] = value
    return out


def reference(
    x, c, ctx, c_ctx, ada_w, ada_b, ffn1_w_gu, ffn1_w_down, w_in, q_gain, k_gain, pool_w,
    pool_scale, fft_w, w_out, ffn2_w_gu, ffn2_w_down, final_gain, norm_mix_g_2, norm_mlp_g_2,
    final_norm_g_2, a_w_in_2, a_conv_w_2, a_conv_b_2, a_gate_a_w_2, a_gate_a_b_2, a_gate_x_w_2,
    a_gate_x_b_2, a_lambda_2, a_w_out_2, b_w_in_2, b_norm_g_2, b_w_s_2, b_s_bias_2, b_w_out_2,
    c_w_in_2, c_conv_w_2, c_w_out_2, mlp_w1_2, mlp_w2_2,
):
    x = first_block(
        x, c, ctx, c_ctx, ada_w, ada_b, ffn1_w_gu, ffn1_w_down, w_in, q_gain, k_gain, pool_w,
        pool_scale, fft_w, w_out, ffn2_w_gu, ffn2_w_down, final_gain,
    )
    return second_block(
        x, norm_mix_g_2, norm_mlp_g_2, final_norm_g_2, a_w_in_2, a_conv_w_2, a_conv_b_2,
        a_gate_a_w_2, a_gate_a_b_2, a_gate_x_w_2, a_gate_x_b_2, a_lambda_2, a_w_out_2, b_w_in_2,
        b_norm_g_2, b_w_s_2, b_s_bias_2, b_w_out_2, c_w_in_2, c_conv_w_2, c_w_out_2, mlp_w1_2,
        mlp_w2_2,
    )


_drawn_inputs = setup_inputs


def setup_inputs(seed=0):
    import zlib

    import numpy as np

    out = dict(_drawn_inputs(seed))
    spreads = {}
    factors = {'q_gain': 8.0, 'k_gain': 8.0, 'a_gate_a_b_2': 4.355}
    for name, (base, spread) in spreads.items():
        noise = np.random.default_rng([zlib.crc32(name.encode()), seed]).standard_normal(out[name].shape)
        drawn = base * np.exp(spread * noise) if base else spread * noise
        out[name] = __import__('jax').numpy.asarray(drawn.astype(out[name].dtype))
    for name, factor in factors.items():
        out[name] = (out[name] * factor).astype(out[name].dtype)
    return out
```

```python
from contextlib import ExitStack

import numpy as np

import concourse.bass as bass
from concourse import mybir

F32 = mybir.dt.float32
F32R = mybir.dt.float32r
ACT = mybir.ActivationFunctionType
ALU = mybir.AluOpType
AX = mybir.AxisListType

P = 128
D = 1024
KD = D // P
S = 256
T = 2 * S
DEPTH = 2
N_MOD = 9
D_FF = 2816
NF = D_FF // P
D_MLP = 4096
NM = D_MLP // P
IN_TILES = 10
HD = 64
D_RNN = 1280
NR = D_RNN // P
A_HD = 80
EPS = 1e-6
ATTN_SCALE = HD ** -0.5
GRID_W = 64
RING = 4
SLOT = 1024
PADW = 272

PLAN = [("ada_head", 16)]
for _l in range(DEPTH):
    PLAN.append((f"ffn1_up{_l}", 2 * NF + (40 if _l == 0 else 32)))
    PLAN.append((f"ffn1_down{_l}", NF))
    PLAN.append((f"in{_l}", IN_TILES))
    if _l == 0:
        PLAN.append(("ada_mid", 16))
    PLAN.append((f"out{_l}", KD))
    PLAN.append((f"ffn2_up{_l}", 2 * NF + (40 if _l == 0 else 0)))
    PLAN.append((f"ffn2_down{_l}", NF))
MIXERS = ["rglru", "sgu", "conv", "rglru"]
UP2 = {"rglru": 2 * NR, "sgu": 2 * KD, "conv": 3 * KD}
DOWN2 = {"rglru": NR, "sgu": KD, "conv": KD}
for _i, _kind in enumerate(MIXERS):
    PLAN += [(f"b_in{_i}", UP2[_kind]), (f"b_out{_i}", DOWN2[_kind]),
             (f"mlp_up{_i}", NM), (f"mlp_down{_i}", NM)]
START = {}
_n = 0
for _name, _k in PLAN:
    START[_name] = _n
    _n += _k
N_SLOTS = _n
assert N_SLOTS % RING == 0

LAST_EPOCH = 1 + 3 * DEPTH + 1 + 2 * len(MIXERS)
SMALL = {0: 16, 1: 48, 3: 64}

ADA_ORDER = ([(0, 0), (0, 1)] + [(0, g) for g in range(2, 7)] + [(0, 7), (0, 8)]
             + [(1, g) for g in range(9)])

GATE_K = {m: [k for k in range(max(0, m - 1), min(NR, m + 2))
              if any(h * A_HD < (k + 1) * P and (h + 1) * A_HD > k * P
                     and h * A_HD < (m + 1) * P and (h + 1) * A_HD > m * P
                     for h in range(D_RNN // A_HD))] for m in range(NR)}

VEC = {}
_n = 0
for _name, _k in [("final1", KD), ("final2", KD), ("norm_mix", 4 * KD), ("norm_mlp", 4 * KD),
                  ("conv_w", 2 * 4 * NR), ("conv_b", 2 * NR), ("ba", 2 * NR), ("bx", 2 * NR),
                  ("lam", 2 * NR), ("b_norm", KD), ("c_conv", 3 * KD),
                  ("q_gain", DEPTH), ("k_gain", DEPTH), ("pool_scale", 2 * DEPTH)]:
    VEC[_name] = _n
    _n += _k
N_VEC = _n

CST = {}
_n = 0
for _name, _k in [("cos", S), ("sin", S), ("dft_c", 2 * P), ("dft_s", 4 * S), ("inv_cnt", 2 * S),
                  ("swap", P), ("blk", P)]:
    CST[_name] = _n
    _n += _k
N_CST = _n


class Tally(dict):

    def __missing__(self, key):
        return 0


def build(nc, x_in, stream, vec_in, cvec_in, ada_b_in, cst_in, small_in, fftw_in, poolw_in,
          gate_in, ws_in, sb_in, out):
    with ExitStack() as ctx:
        def sem(name):
            return ctx.enter_context(nc.semaphore(name))

        place = [nc.sbuf_base]

        def sb(name, shape, dt=F32):
            size = 4 * int(np.prod(shape[1:]))
            off = (place[0] + 31) // 32 * 32
            place[0] = off + size
            assert place[0] <= nc.sbuf_usable_end, (name, place[0])
            return nc.alloc_sbuf_tensor_at(name, shape, dt, offset=off)

        X = sb("X", [P, KD, T])
        raw = sb("raw", [P, RING, SLOT])
        whi = sb("whi", [P, RING, SLOT], F32R)
        wlo = sb("wlo", [P, RING, SLOT], F32R)
        tmpa = sb("tmpa", [P, 2, T])
        tmpb = sb("tmpb", [P, 2, T])
        rstd = sb("rstd", [P, T])
        ones = sb("ones", [P, P])
        ident = sb("ident", [P, P])
        vec = sb("vec", [P, N_VEC])
        common = place[0]
        nh = sb("nh", [P, KD, T], F32R)
        nl = sb("nl", [P, KD, T], F32R)
        cst4 = sb("cst4", [P, 8 * 4 + 124], F32R)
        csil = sb("csil", [P, KD, 2])
        cvec = sb("cvec", [P, KD, 2])
        sel4 = sb("sel4", [4, 2])
        ada_row = sb("ada_row", [4, SLOT])
        mod = sb("mod", [P, DEPTH * N_MOD, KD, 2])
        ada_b = sb("ada_b", [P, DEPTH * N_MOD, KD, 2])
        fix = sb("fix", [P, DEPTH * 5, KD, 2])
        mixer = place[0]
        hh = sb("hh", [P, NF * T], F32R)
        hl = sb("hl", [P, NF * T], F32R)
        place[0] = mixer
        cst = sb("cst", [P, N_CST])
        fftw = sb("fftw", [P, 2, 2 * P])
        poolw = sb("poolw", [P, 2, P])
        kq = sb("kq", [P, T + 4 * T])
        kqs = sb("kqs", [P, T + 4 * T])
        zv = sb("zv", [P, T])
        zf = sb("zf", [P, 2, T])
        vtok = sb("vtok", [P, 4, P])
        rot = sb("rot", [P, 2, S])
        up = sb("up", [P, 2, 2, PADW])
        pc = sb("pc", [P, 2, 2, S])
        yt = sb("yt", [P, 2, T])
        ab = sb("ab", [P, 4, 2, 2 * P])
        smx = sb("smx", [P, 32])
        snm = sb("snm", [P, 32])
        ssm = sb("ssm", [P, 32])
        srs = sb("srs", [P, 32])
        scratch = place[0]
        w2 = sb("w2", [P, 2, 2, PADW])
        w4 = sb("w4", [P, 2, 2, PADW])
        w8 = sb("w8", [P, 2, PADW])
        w16 = sb("w16", [P, 2, PADW])
        place[0] = scratch
        prob = sb("prob", [P, 2, T])
        probT = sb("probT", [P, 2, 4, S])
        assert place[0] <= mixer + 8 * NF * T
        place[0] = common
        bh = sb("bh", [P, NR, S], F32R)
        bl = sb("bl", [P, NR, S], F32R)
        n8sp = sb("n8sp", [P, 2 * NR])
        sp_t = sb("sp_t", [P, 6, 2 * NR])
        nbx = sb("nbx", [P, 4 * NR])
        second = place[0]
        mh = sb("mh", [P, NM * S], F32R)
        ml = sb("ml", [P, NM * S], F32R)
        place[0] = second
        gates_w = sb("gates_w", [P, 2, NR, 3 * P])
        gelu_g = sb("gelu_g", [P, NR, S])
        xpad = sb("xpad", [P, 2, 3 + S])
        cv = sb("cv", [P, NR, S])
        sg = sb("sg", [P, 2, 2 * S])
        av = sb("av", [P, NR, S])
        th = sb("th", [P, NR, S])
        ix = sb("ix", [P, NR, S])
        dd = sb("dd", [P, NR, S])
        place[0] = second
        ws = sb("ws", [P, KD, P])
        sbias = sb("sbias", [1, KD * P])
        vg = sb("vg", [P, KD, S])
        ug = sb("ug", [P, KD, S])
        vn = sb("vn", [P, 2, S])
        vt = sb("vt", [P, KD, S])
        place[0] = second
        cpad = sb("cpad", [P, 2, 2 + S])
        ch = sb("ch", [P, KD, S], F32R)
        cl = sb("cl", [P, KD, S], F32R)

        ps = ctx.enter_context(nc.psum_tensor("ps", [P, 8, T], F32))

        x_loaded = sem("x_loaded")
        vec_loaded = sem("vec_loaded")
        cond_loaded = sem("cond_loaded")
        mix_loaded = sem("mix_loaded")
        raw_loaded = [sem(f"raw_loaded{r}") for r in range(RING)]
        w_hi_ready = sem("w_hi_ready")
        w_ready = sem("w_ready")
        slots_done = sem("slots_done")
        acc_done = sem("acc_done")
        x_new = sem("x_new")
        sq_ready = sem("sq_ready")
        sq_summed = sem("sq_summed")
        recip_done = sem("recip_done")
        rstd_ready = sem("rstd_ready")
        y_ready = sem("y_ready")
        nh_ready = sem("nh_ready")
        nl_ready = sem("nl_ready")
        up_act = sem("up_act")
        up_evac = sem("up_evac")
        hid_hi = sem("hid_hi")
        hid_lo = sem("hid_lo")
        csil_ready = sem("csil_ready")
        c_hi_ready = sem("c_hi_ready")
        c_ready = sem("c_ready")
        ada_done = sem("ada_done")
        ada_row_ready = sem("ada_row_ready")
        ada_cols_done = sem("ada_cols_done")
        mod_ready = sem("mod_ready")
        dve_chain = sem("dve_chain")
        act_chain = sem("act_chain")
        pool_chain = sem("pool_chain")
        consts_ready = sem("consts_ready")
        pads_ready = sem("pads_ready")
        z_ready = sem("z_ready")
        hssq_done = sem("hssq_done")
        hms_read = sem("hms_read")
        hrecip = sem("hrecip")
        hrstd = sem("hrstd")
        zn_ready = sem("zn_ready")
        rot_done = sem("rot_done")
        qk_ready = sem("qk_ready")
        vt_done = sem("vt_done")
        vtok_ready = sem("vtok_ready")
        f1_done = sem("f1_done")
        ab_ready = sem("ab_ready")
        f2_done = sem("f2_done")
        yt_ready = sem("yt_ready")
        pool_in = sem("pool_in")
        pool_ready = sem("pool_ready")
        side_done = sem("side_done")
        side_hi = sem("side_hi")
        side_lo = sem("side_lo")
        s_done = sem("s_done")
        nmax_ready = sem("nmax_ready")
        exp_ready = sem("exp_ready")
        prob_ready = sem("prob_ready")
        pt_done = sem("pt_done")
        pts_ready = sem("pts_ready")
        o_done = sem("o_done")
        o_hi = sem("o_hi")
        o_lo = sem("o_lo")
        sp_step = sem("sp_step")
        b_evac = sem("b_evac")
        b_pad = sem("b_pad")
        b_f32 = sem("b_f32")
        b_hi = sem("b_hi")
        b_lo = sem("b_lo")
        cv_ready = sem("cv_ready")
        gate_mm = sem("gate_mm")
        gate_exp = sem("gate_exp")
        gate_sig = sem("gate_sig")
        gate_ab = sem("gate_ab")
        rad_ready = sem("rad_ready")
        root_ready = sem("root_ready")
        small_loaded = sem("small_loaded")
        ws_ready = sem("ws_ready")
        vn_ready = sem("vn_ready")
        vtt_done = sem("vtt_done")
        vtt_ready = sem("vtt_ready")
        mixd_done = sem("mixd_done")
        out_sem = sem("out_sem")

        def vcol(name, i):
            return vec[:, VEC[name] + i:VEC[name] + i + 1]

        def ccol(name, a, b):
            return cst[:, CST[name] + a:CST[name] + b]

        def bank(b, w=T):
            return ps[:, b, 0:w]

        def kq_at(i, w):
            return (0, T) if i == 0 else (T + (i - 1) * w, w)

        def mix_w(l):
            return T if l == 0 else S

        def attn_units(l):
            units = []
            g = 0
            for t in range(4):
                for s in range(1 if l else 2):
                    for h2 in range(2):
                        for qt in range(2):
                            units.append((g, s, t, h2, qt, range(4) if s == 0 else range(2, 4)))
                    g += 1
            return units

        IN_BANK = [i % 8 for i in range(IN_TILES)]
        OUT_K = [4, 5, 6, 7, 0, 1, 2, 3]

        block = ctx.enter_context(nc.Block())

        @block.sync
        def _(sp):
            sp.dma_start(cvec[:], cvec_in).then_inc(cond_loaded, 16)
            sp.dma_start(ada_b[:], ada_b_in).then_inc(cond_loaded, 16)
            sp.dma_start(sel4[:], small_in[0:4, 0:2]).then_inc(cond_loaded, 16)
            for r in range(RING):
                sp.dma_start(raw[:, r, :], stream[r]).then_inc(raw_loaded[r], 16)
            sp.dma_start(X[:], x_in).then_inc(x_loaded, 16)
            sp.dma_start(vec[:], vec_in).then_inc(vec_loaded, 16)
            sp.dma_start(ident[:], small_in[:, 2:2 + P]).then_inc(vec_loaded, 16)
            with sp.Fori(1, N_SLOTS // RING) as i:
                for r in range(RING):
                    sp.wait_ge(w_ready, i * RING + (r + 1 - RING))
                    sp.dma_start(raw[:, r, :], stream[bass.ds(i * RING + r, 1), :, :].rearrange("a p n -> (a p) n")
                                 ).then_inc(raw_loaded[r], 16)
            for m in range(KD):
                sp.wait_ge(x_new, LAST_EPOCH * KD + m + 1)
                sp.dma_start(out[:, m, :], X[:, m, 0:S]).then_inc(out_sem, 16)
            sp.wait_ge(out_sem, 16 * KD)

        @block.tensor
        def _(pe):
            c = Tally()
            pe.sem_inc(slots_done, RING)

            def weights(at, dyn=0):
                pe.wait_ge(w_ready, dyn + (at + 1))

            def mm3(dst, at, tile, rhs_hi, rhs_lo, start, stop):
                r = at % RING
                w1 = whi[:, r, tile * P:(tile + 1) * P]
                w2 = wlo[:, r, tile * P:(tile + 1) * P]
                pe.matmul(dst, w1, rhs_hi, start=start, stop=False)
                pe.matmul(dst, w1, rhs_lo, start=False, stop=False)
                return pe.matmul(dst, w2, rhs_hi, start=False, stop=stop)

            def norm(w, split=True):
                for m in range(KD):
                    pe.wait_ge(sq_ready, c["sq"] + m + 1)
                    pe.matmul(bank(0, w), ones[:], tmpa[:, m % 2, 0:w], start=(m == 0),
                              stop=(m == KD - 1)).then_inc(sq_summed, 1)
                c["sq"] += KD
                c["nl"] += KD if split else 0

            def out_tile(dst, at, dyn, w, src_h, src_l, first=False):
                weights(at, dyn)
                for k in range(KD):
                    if first:
                        pe.wait_ge(nl_ready, c["nl"] - KD + k + 1)
                    last = mm3(dst, at, k, src_h[:, k, 0:w], src_l[:, k, 0:w], k == 0, k == KD - 1)
                last.then_inc(slots_done, 1)

            def up4(at, dyn, unit, udyn, w, mlp):
                for u in range(2):
                    pe.wait_ge(up_evac, udyn + (unit + u + 1))
                    for half in range(2):
                        if mlp:
                            dst = ps[:, u, half * S:(half + 1) * S]
                        else:
                            dst = bank(2 * u + half, w)
                        src_h, src_l = (bh, bl) if mlp else (nh, nl)
                        out_tile(dst, at + 2 * u + half, dyn, w, src_h, src_l,
                                 first=(u == 0 and half == 0))

            def ada4(at, dyn, half):
                for q in range(4):
                    weights(at + q, dyn)
                    kt = half * 4 + q
                    r = (at + q) % RING
                    for b in range(2):
                        for w in (whi, wlo):
                            last = pe.matmul(bank(4 + b), cst4[:, 4 * kt:4 * kt + P],
                                             w[:, r, b * 512:(b + 1) * 512],
                                             start=(kt == 0 and w is whi),
                                             stop=(kt == KD - 1 and w is wlo))
                    last.then_inc(slots_done, 1)

            def ada_cols(g, gdyn):
                pe.wait_ge(ada_row_ready, gdyn + (g + 1))
                if g:
                    pe.wait_ge(mod_ready, gdyn + g)
                for m in range(KD):
                    last = pe.matmul(ps[:, 6, 2 * m:2 * m + 2], ada_row[:, m * P:(m + 1) * P],
                                     sel4[:], start=True, stop=True)
                last.then_inc(ada_cols_done, 1)

            def ffn_up(name, w, ada_groups):
                at = START[name]
                if ada_groups:
                    with pe.Fori(0, ada_groups) as i:
                        if c["ada"]:
                            pe.wait_ge(ada_row_ready, i + c["ada"])
                        ada4(at, i * 16, 0)
                        up4(at + 4, i * 16, c["unit"], i * 4, w, False)
                        ada4(at + 8, i * 16, 1)
                        up4(at + 12, i * 16, c["unit"] + 2, i * 4, w, False)
                        ada_cols(c["ada"], i)
                    at += 16 * ada_groups
                    c["unit"] += 4 * ada_groups
                    c["ada"] += ada_groups
                left = (START[name.replace("up", "down")] - at) // 4
                with pe.Fori(0, left) as i:
                    up4(at, i * 4, c["unit"], i * 2, w, False)
                c["unit"] += 2 * left

            def mlp_up(name):
                with pe.Fori(0, NM // 4) as i:
                    up4(START[name], i * 4, c["unit"], i * 2, S, True)
                c["unit"] += NM // 2

            def down_slot(at, dyn, k, kdyn, w, src_h, src_l, ready, first, last, per_unit=1):
                weights(at, dyn)
                if ready is not None:
                    pe.wait_ge(*ready)
                order = [4, 5, 6, 7, 0, 1, 2, 3] if first else range(KD)
                for n, m in enumerate(order):
                    if first and n == 4:
                        pe.wait_ge(up_evac, c["unit"] + 1)
                    if first and n == 4 + 2 // per_unit:
                        pe.wait_ge(up_evac, c["unit"] + 2)
                    ins = mm3(bank(m, w), at, m, src_h(k, kdyn), src_l(k, kdyn), first, last)
                    if last and m < KD - 1:
                        ins.then_inc(acc_done, 1)
                ins.then_inc(slots_done, 1)

            def down(name, n_k, w, src_h, src_l, per_unit):
                at = START[name]
                pe.wait_ge(mod_ready, c["ada"]) if c["ada"] and not c["block2"] else None
                base = c["hid"]

                def ready(k, kdyn):
                    return (hid_lo, kdyn + (base + k // per_unit + 3))

                for k in range(4):
                    down_slot(at + k, 0, k, 0, w, src_h, src_l, ready(k, 0), k == 0, False,
                              per_unit)
                tail = n_k % 4 or 4
                loops = (n_k - 4 - tail) // 4
                with pe.Fori(0, loops) as i:
                    for q in range(4):
                        down_slot(at + 4 + q, i * 4, 4 + q, i, w, src_h, src_l,
                                  ready(4 + q, i * (4 // per_unit)), False, False)
                for k in range(n_k - tail, n_k):
                    down_slot(at + k, 0, k, 0, w, src_h, src_l, ready(k, 0), False, k == n_k - 1)
                c["hid"] += n_k // per_unit

            def hid(buf, step, w):
                def at(k, kdyn):
                    if isinstance(kdyn, int):
                        return buf[:, k * step:k * step + w]
                    return buf[:, bass.ds(kdyn * (4 * step) + k * step, w)]
                return at

            def short_down(name, w, src_h, src_l, order, readies):
                at = START[name]
                for n, k in enumerate(order):
                    weights(at + n)
                    pe.wait_ge(*readies[n])
                    last = n == len(order) - 1
                    for m in range(KD):
                        ins = mm3(bank(m, w), at + n, m, src_h[:, k, 0:w], src_l[:, k, 0:w], n == 0, last)
                        if last and m < KD - 1:
                            ins.then_inc(acc_done, 1)
                    ins.then_inc(slots_done, 1)

            def attention(l):
                units = attn_units(l)
                w = mix_w(l)
                n = len(units)

                def scores(u):
                    g, s, t, h2, qt, kts = units[u]
                    if u >= 2:
                        pe.wait_ge(exp_ready, c["att"] + u - 1)
                    a, _ = kq_at(1 + t, w)
                    rows = slice(64 * h2, 64 * h2 + 64)
                    keys = slice(kts[0] * P, (kts[-1] + 1) * P)
                    nk = len(kts) * P
                    pe.matmul(ps[:, u % 2, 0:nk], kq[rows, a + s * S + qt * P:a + s * S + (qt + 1) * P],
                              kq[rows, keys], start=True, stop=True).then_inc(s_done, 1)

                def values(pair):
                    g, s, t, h2, _, kts = units[2 * pair]
                    pe.wait_ge(pts_ready, c["att"] + 2 * pair + 2)
                    if g >= 2:
                        pe.wait_ge(o_lo, c["og"] + g - 1)
                    for n_, kt in enumerate(kts):
                        last = pe.matmul(ps[64 * h2:64 * h2 + 64, 4 + g % 2, 0:S],
                                         vtok[:, kt, 64 * h2:64 * h2 + 64], probT[:, pair % 2, kt, :],
                                         start=(n_ == 0), stop=(n_ == len(kts) - 1))
                    last.then_inc(o_done, 1)

                pe.wait_ge(qk_ready, 5 * (l + 1))
                pe.wait_ge(vtok_ready, l + 1)
                pe.wait_ge(side_lo, 4 * (l + 1))
                scores(0)
                for u in range(n):
                    if u + 1 < n:
                        scores(u + 1)
                    if u >= 2:
                        pe.wait_ge(pts_ready, c["att"] + u - 1)
                    pe.wait_ge(prob_ready, c["att"] + u + 1)
                    kts = units[u][5]
                    for j in range(len(kts)):
                        last = pe.transpose(ps[:, 2 + u % 2, j * P:(j + 1) * P],
                                            prob[:, u % 2, j * P:(j + 1) * P], ident[:])
                    last.then_inc(pt_done, 1)
                    if u % 2 == 0 and u:
                        values(u // 2 - 1)
                values(n // 2 - 1)
                c["att"] += n
                c["og"] += n // 4

            def mixer1(l):
                at = START[f"in{l}"]
                w = mix_w(l)
                for i in range(8):
                    out_tile(bank(IN_BANK[i], T if i < 2 else w), at + i, 0, T if i < 2 else w, nh, nl,
                             first=(i == 0))
                pe.wait_ge(mix_loaded, 48 * (l + 1))
                pe.wait_ge(z_ready, 10 * l + 7)
                for i in range(5):
                    a, ww = kq_at(i, w)
                    pe.matmul(bank(2 + i, ww), ccol("blk", 0, P), kqs[:, a:a + ww], start=True,
                              stop=True).then_inc(hssq_done, 1)
                for i in range(8, IN_TILES):
                    out_tile(bank(IN_BANK[i], w), at + i, 0, w, nh, nl)
                if l == 0:
                    at = START["ada_mid"]
                    pe.wait_ge(hms_read, 1)
                    for g in range(2):
                        if g:
                            pe.wait_ge(ada_row_ready, c["ada"])
                        ada4(at + 8 * g, 0, 0)
                        ada4(at + 8 * g + 4, 0, 1)
                        ada_cols(c["ada"], 0)
                        c["ada"] += 1
                pe.wait_ge(z_ready, 10 * l + 10)
                for kt in range(4):
                    last = pe.transpose(ps[:, 7, kt * P:(kt + 1) * P], zv[:, kt * P:(kt + 1) * P], ident[:])
                last.then_inc(vt_done, 1)
                for u in range(2 * (w // S)):
                    if u >= 2:
                        pe.wait_ge(ab_ready, c["f1"] + u - 1)
                    for ch in range(2):
                        last = pe.matmul(ps[:, u % 2, ch * 2 * P:(ch + 1) * 2 * P],
                                         zf[:, ch, u * P:(u + 1) * P], ccol("dft_c", 0, 2 * P),
                                         start=True, stop=True)
                    last.then_inc(f1_done, 1)
                pe.wait_ge(hms_read, l + 1)
                for s in range(w // S):
                    pe.wait_ge(ab_ready, c["f1"] + 2 * s + 2)
                    for ch in range(2):
                        for tt in range(2):
                            for cs in range(2):
                                o = (tt * 2 + cs) * S
                                last = pe.matmul(bank(2 + 2 * s + ch, S),
                                                 ab[:, 2 * s + tt, ch, cs * P:(cs + 1) * P],
                                                 ccol("dft_s", o, o + S), start=(tt == 0 and cs == 0),
                                                 stop=(tt == 1 and cs == 1))
                        last.then_inc(f2_done, 1)
                c["f1"] += 2 * (w // S)
                c["f2"] += 2 * (w // S)
                pe.wait_ge(yt_ready, c["f2"])
                if l == 0:
                    pe.wait_ge(mod_ready, c["ada"])
                pe.wait_ge(vtok_ready, l + 1)
                for m in range(2):
                    for k in range(2):
                        last = pe.matmul(bank(6 + m, w), fftw[:, k, m * P:(m + 1) * P], yt[:, k, 0:w],
                                         start=(k == 0), stop=(k == 1))
                    last.then_inc(side_done, 1)
                pe.wait_ge(ab_ready, c["f1"])
                pe.wait_ge(pool_ready, l + 1)
                for m in range(2):
                    pe.matmul(bank(m, w), poolw[:, m, :], pc[:, m, 0:w // S, :], start=True,
                              stop=True).then_inc(side_done, 1)
                pe.wait_ge(zn_ready, 2 * (l + 1))
                pe.wait_ge(side_lo, 4 * l + 2)
                for i in range(5):
                    a, _ = kq_at(i, w)
                    pe.matmul(bank(2 + i, S), ccol("swap", 0, P), kq[:, a:a + S], start=True,
                              stop=True).then_inc(rot_done, 1)
                attention(l)
                readies = ([(side_lo, 4 * (l + 1))] * 4
                           + [(o_lo, c["og"] - (w // S) * (3 - t)) for t in range(4)])
                pe.wait_ge(o_lo, c["og"])
                short_down(f"out{l}", w, nh, nl, OUT_K, readies)

            pe.wait_ge(consts_ready, 1)
            pe.wait_ge(cond_loaded, 48)
            pe.wait_ge(c_ready, 1)
            for g in range(2):
                if g:
                    pe.wait_ge(ada_row_ready, 1)
                ada4(8 * g, 0, 0)
                ada4(8 * g + 4, 0, 1)
                ada_cols(g, 0)
                c["ada"] += 1
            for l in range(DEPTH):
                norm(T)
                ffn_up(f"ffn1_up{l}", T, 5 if l == 0 else 4)
                down(f"ffn1_down{l}", NF, T, hid(hh, T, T), hid(hl, T, T), 1)
                norm(T)
                mixer1(l)
                w = mix_w(l)
                norm(w)
                ffn_up(f"ffn2_up{l}", w, 5 if l == 0 else 0)
                down(f"ffn2_down{l}", NF, w, hid(hh, T, w), hid(hl, T, w), 1)
            c["block2"] = 1
            norm(S, split=False)

            def rglru(i, j):
                at = START[f"b_in{i}"]
                for m in range(2 * NR):
                    if m >= 6:
                        pe.wait_ge(b_evac, c["bev"] + m - 5)
                    out_tile(bank(m % 6, S), at + m, 0, S, bh, bl, first=(m == 0))
                c["bev"] += 2 * NR
                pe.wait_ge(b_evac, c["bev"])
                pe.wait_ge(small_loaded, SMALL[i])
                for m in range(NR):
                    pe.wait_ge(cv_ready, c["cv"] + min(NR, m + 2))
                    if m >= 4:
                        pe.wait_ge(gate_exp, c["gex"] + m - 3)
                    for g in range(2):
                        for n, k in enumerate(GATE_K[m]):
                            o = (m - k + 1) * P
                            last = pe.matmul(ps[:, m % 4, g * S:(g + 1) * S], gates_w[:, g, k, o:o + P],
                                             cv[:, k, :], start=(n == 0), stop=(n == len(GATE_K[m]) - 1))
                    last.then_inc(gate_mm, 1)
                c["cv"] += NR
                c["gex"] += NR
                pe.wait_ge(gate_exp, c["gex"])
                short_down(f"b_out{i}", S, bh, bl, range(NR), [(b_lo, c["blo"] + k + 1) for k in range(NR)])
                c["blo"] += NR

            def sgu(i):
                at = START[f"b_in{i}"]
                for m in range(2 * KD):
                    if m >= 6:
                        pe.wait_ge(b_evac, c["bev"] + m - 5)
                    out_tile(bank(m % 6, S), at + m, 0, S, bh, bl, first=(m == 0))
                    if 1 <= m <= KD:
                        pe.wait_ge(sq_ready, c["sq"] + m)
                        pe.matmul(bank(7, S), ones[:], tmpa[:, (m - 1) % 2, 0:S], start=(m == 1),
                                  stop=(m == KD)).then_inc(sq_summed, 1)
                c["sq"] += KD
                c["bev"] += 2 * KD
                pe.wait_ge(b_evac, c["bev"])
                pe.wait_ge(ws_ready, 1)
                pe.wait_ge(small_loaded, SMALL[i])

                def turn(m):
                    pe.wait_ge(vn_ready, m + 1)
                    if m >= 2:
                        pe.wait_ge(vtt_ready, m - 1)
                    for n in range(2):
                        last = pe.transpose(ps[:, 2 + m % 2, n * P:(n + 1) * P], vn[:, m % 2, n * P:(n + 1) * P],
                                            ident[:])
                    last.then_inc(vtt_done, 1)

                turn(0)
                for m in range(KD):
                    if m + 1 < KD:
                        turn(m + 1)
                    pe.wait_ge(vtt_ready, m + 1)
                    if m >= 2:
                        pe.wait_ge(b_f32, c["blo"] + m - 1)
                    for n in range(2):
                        dst = ps[:, m % 2, n * P:(n + 1) * P]
                        pe.matmul(dst, vt[:, m, n * P:(n + 1) * P], ws[:, m, :], start=True, stop=False)
                        last = pe.matmul(dst, ones[0:1, :], sbias[:, m * P:(m + 1) * P], start=False, stop=True)
                    last.then_inc(mixd_done, 1)
                pe.wait_ge(b_f32, c["blo"] + KD)
                short_down(f"b_out{i}", S, bh, bl, range(KD), [(b_lo, c["blo"] + k + 1) for k in range(KD)])
                c["blo"] += KD

            def conv(i):
                at = START[f"b_in{i}"]
                for m in range(KD):
                    if m >= 2:
                        pe.wait_ge(b_f32, c["blo"] + m - 1)
                    for q in range(3):
                        out_tile(bank(3 * (m % 2) + q, S), at + 3 * m + q, 0, S, bh, bl,
                                 first=(m == 0 and q == 0))
                c["bev"] += KD
                pe.wait_ge(b_f32, c["blo"] + KD)
                short_down(f"b_out{i}", S, ch, cl, range(KD), [(b_lo, c["blo"] + k + 1) for k in range(KD)])
                c["blo"] += KD

            for i, kind in enumerate(MIXERS):
                norm(S)
                if kind == "rglru":
                    rglru(i, i // 3)
                elif kind == "sgu":
                    sgu(i)
                else:
                    conv(i)
                norm(S)
                mlp_up(f"mlp_up{i}")
                down(f"mlp_down{i}", NM, S, hid(mh, S, S), hid(ml, S, S), 2)
            norm(S, split=False)

        @block.scalar
        def _(act):
            c = Tally()

            def split(at, dyn=0):
                if at >= N_SLOTS:
                    return
                r = at % RING
                act.wait_ge(raw_loaded[r], dyn * 4 + 16 * (at // RING + 1))
                act.wait_ge(slots_done, dyn + (at + 1))
                act.activation(whi[:, r, :], raw[:, r, :], ACT.Copy).then_inc(w_hi_ready, 1)

            def split_to(at):
                while c["split"] <= at:
                    split(c["split"])
                    c["split"] += 1

            def done(at, dyn=0):
                act.wait_ge(slots_done, dyn + (RING + at + 1))

            def norm(w, ord_shift=None, dst=None, bias=True, split_out=True):
                act.preload_act_table(ACT.Sqrt)
                for m in range(KD):
                    act.wait_ge(x_new, c["x"] + m + 1)
                    if m >= 2:
                        act.wait_ge(sq_summed, c["sq"] + m - 1)
                    act.activation(tmpa[:, m % 2, 0:w], X[:, m, 0:w], ACT.Square).then_inc(sq_ready, 1)
                c["x"] += KD
                c["sq"] += KD
                root(w)
                if not split_out:
                    return
                if bias:
                    act.wait_ge(mod_ready, ord_shift + 1)
                for m in range(KD):
                    act.wait_ge(y_ready, c["y"] + m + 1)
                    if bias:
                        for s in range(w // S):
                            last = act.activation(dst[:, m, s * S:(s + 1) * S], tmpb[:, m % 2, s * S:(s + 1) * S],
                                                  ACT.Identity, bias=mod[:, ord_shift, m, s:s + 1])
                    else:
                        last = act.activation(dst[:, m, 0:w], tmpb[:, m % 2, 0:w], ACT.Copy)
                    last.then_inc(nh_ready, 1)
                c["y"] += KD

            def root(w):
                c["rms"] += 1
                act.wait_ge(recip_done, c["rms"])
                act.activation(rstd[:, 0:w], tmpb[:, 1, 0:w], ACT.Sqrt).then_inc(rstd_ready, 1)

            def unit(at, dyn, u, udyn, w, mlp, local, ldyn):
                done(at + 1 if mlp else at, dyn)
                act.wait_ge(up_evac, udyn + (u + 1))
                if mlp:
                    act.activation(tmpa[:, u % 2, :], ps[:, u % 2, :], ACT.Relu).then_inc(up_act, 1)
                    w, dst = T, mh
                else:
                    act.activation(tmpa[:, u % 2, 0:w], bank(2 * (u % 2), w), ACT.Silu).then_inc(up_act, 1)
                    dst = hh
                act.wait_ge(up_evac, udyn + (u + 3))
                act.activation(dst[:, bass.ds(ldyn * T + local * T, w)], tmpb[:, u % 2, 0:w],
                               ACT.Copy).then_inc(hid_hi, 1)

            def up4(at, dyn, u, udyn, w, mlp, local, ldyn):
                for q in range(2):
                    split(at + 3 + 2 * q, dyn)
                    split(at + 4 + 2 * q, dyn)
                    unit(at + 2 * q, dyn, u + q, udyn, w, mlp, local + q, ldyn)

            def ada_rows(g, gdyn):
                if g:
                    act.wait_ge(ada_cols_done, gdyn + g)
                act.activation(ada_row[:].rearrange("p (a b) -> p a b", a=2), ps[0:4, 4:6, :],
                               ACT.Copy).then_inc(ada_row_ready, 1)

            def ffn_up(name, w, ada_groups):
                at = START[name]
                act.preload_act_table(ACT.Silu)
                local = 0
                if ada_groups:
                    with act.Fori(0, ada_groups) as i:
                        for q in range(4):
                            split(at + 3 + q, i * 16)
                        up4(at + 4, i * 16, c["unit"], i * 4, w, False, 0, i * 4)
                        for q in range(4):
                            split(at + 11 + q, i * 16)
                        done(at + 11, i * 16)
                        ada_rows(c["ada"], i)
                        up4(at + 12, i * 16, c["unit"] + 2, i * 4, w, False, 2, i * 4)
                    at += 16 * ada_groups
                    c["unit"] += 4 * ada_groups
                    c["ada"] += ada_groups
                    local = 4 * ada_groups
                left = (START[name.replace("up", "down")] - at) // 4
                with act.Fori(0, left) as i:
                    up4(at, i * 4, c["unit"], i * 2, w, False, local, i * 2)
                c["unit"] += 2 * left
                c["split"] = at + 4 * left + 3

            def mlp_up(name):
                with act.Fori(0, NM // 4) as i:
                    up4(START[name], i * 4, c["unit"], i * 2, S, True, 0, i * 2)
                c["unit"] += NM // 2
                c["split"] = START[name] + NM + 3

            def down(name, n_k):
                at = START[name]
                loops = n_k // 4 - 1
                with act.Fori(0, loops) as i:
                    for q in range(4):
                        split(at + 3 + q, i * 4)
                c["split"] = at + 3 + 4 * loops
                split_to(at + n_k + 2)

            def short_down(name, n_k):
                split_to(START[name] + n_k + 2)

            def attention(l):
                units = attn_units(l)
                n = len(units)

                def turned(u):
                    pair, (g, s, t, h2, qt, kts) = u // 2, units[u]
                    act.wait_ge(pt_done, c["att"] + u + 1)
                    if pair >= 2:
                        act.wait_ge(o_done, c["op"] + pair - 1)
                    act.activation(probT[:, pair % 2, kts[0]:kts[-1] + 1, qt * P:(qt + 1) * P],
                                   ps[:, 2 + u % 2, 0:len(kts) * P].rearrange("p (k q) -> p k q", q=P),
                                   ACT.Copy).then_inc(pts_ready, 1)

                def o_upper(g):
                    _, s, t, *_ = units[4 * g]
                    act.wait_ge(o_done, c["op"] + 2 * g + 2)
                    act.activation(nh[:, t, s * S:(s + 1) * S], bank(4 + g % 2, S), ACT.Copy).then_inc(o_hi, 1)

                for u, (g, s, t, h2, qt, kts) in enumerate(units):
                    nk = len(kts) * P
                    act.wait_ge(nmax_ready, c["att"] + u + 1)
                    if u >= 2:
                        act.wait_ge(pt_done, c["att"] + u - 1)
                    act.activation(prob[:, u % 2, 0:nk], ps[:, u % 2, 0:nk], ACT.Exp, bias=snm[:, u:u + 1],
                                   scale=ATTN_SCALE, accum_out=ssm[:, u:u + 1]).then_inc(exp_ready, 1)
                    if u:
                        turned(u - 1)
                    if u >= 5 and u % 4 == 1:
                        o_upper(u // 4 - 1)
                turned(n - 1)
                o_upper(n // 4 - 1)
                c["att"] += n
                c["op"] += n // 2

            def mixer1(l):
                at = START[f"in{l}"]
                w = mix_w(l)
                for i in range(IN_TILES):
                    split_to(at + i + 3)
                    done(at + i)
                    ww = T if i < 2 else w
                    src = bank(IN_BANK[i], ww)
                    if i == 0 or 2 <= i < 6:
                        a, _ = kq_at(i - 1 if i else 0, w)
                        act.activation(kq[:, a:a + ww], src, ACT.Copy)
                        act.activation(kqs[:, a:a + ww], src, ACT.Square).then_inc(z_ready, 1)
                    elif i == 1:
                        act.activation(zv[:], src, ACT.Copy).then_inc(z_ready, 1)
                    elif i < 8:
                        act.wait_ge(pads_ready, l + 1)
                        act.activation(up[:, i - 6, 0:w // S, 8:8 + S], src.rearrange("p (s t) -> p s t", t=S),
                                       ACT.Copy).then_inc(z_ready, 1)
                    else:
                        act.activation(zf[:, i - 8, 0:w], src, ACT.Copy).then_inc(z_ready, 1)
                act.wait_ge(hrecip, l + 1)
                act.activation(kqs[:, 0:T + 4 * w], kqs[:, 0:T + 4 * w], ACT.Sqrt).then_inc(hrstd, 1)
                act.preload_act_table(ACT.Exp)
                if l == 0:
                    at = START["ada_mid"]
                    for g in range(2):
                        split_to(at + 8 * g + 10)
                        done(at + 8 * g + 7)
                        ada_rows(c["ada"], 0)
                        c["ada"] += 1
                act.wait_ge(vt_done, l + 1)
                act.activation(vtok[:].rearrange("p a b -> p (a b)"), bank(7), ACT.Copy).then_inc(vtok_ready, 1)
                for m in range(2):
                    act.wait_ge(side_done, 4 * l + m + 1)
                    act.activation(nh[:, 6 + m, 0:w], bank(6 + m, w), ACT.Copy).then_inc(side_hi, 1)
                for m in range(2):
                    act.wait_ge(side_done, 4 * l + m + 3)
                    act.activation(nh[:, 4 + m, 0:w], bank(m, w), ACT.Identity,
                                   scale=vcol("pool_scale", 2 * l + m)).then_inc(side_hi, 1)
                attention(l)
                short_down(f"out{l}", KD)

            act.wait_ge(cond_loaded, 48)
            act.activation(csil[:].rearrange("p k c -> p (k c)"), cvec[:].rearrange("p k c -> p (k c)"),
                           ACT.Silu).then_inc(csil_ready, 1)
            act.wait_ge(csil_ready, 1)
            act.wait_ge(consts_ready, 1)
            act.activation(cst4[:, 0:32].rearrange("p (k c) -> p k c", c=4)[:, :, 0:2], csil[:],
                           ACT.Copy).then_inc(c_hi_ready, 1)
            for g in range(2):
                split_to(8 * g + 10)
                done(8 * g + 7)
                ada_rows(g, 0)
                c["ada"] += 1
            act.wait_ge(vec_loaded, 32)
            for l in range(DEPTH):
                norm(T, MOD(l, 0), nh)
                ffn_up(f"ffn1_up{l}", T, 5 if l == 0 else 4)
                down(f"ffn1_down{l}", NF)
                norm(T, MOD(l, 3), nh)
                mixer1(l)
                w = mix_w(l)
                norm(w, MOD(l, 6), nh)
                ffn_up(f"ffn2_up{l}", w, 5 if l == 0 else 0)
                down(f"ffn2_down{l}", NF)
            norm(S, split_out=False)
            lam = vec[:, VEC["lam"]:VEC["lam"] + 2 * NR]
            act.wait_ge(x_new, c["x"] + KD)
            act.activation(sp_t[:, 0, :], lam, ACT.Abs).then_inc(act_chain, 1)
            act.wait_ge(act_chain, 1)
            act.activation(sp_t[:, 1, :], sp_t[:, 0, :], ACT.Exp, scale=-1.0).then_inc(sp_step, 1)

            def b_upper(dst, m):
                act.wait_ge(b_f32, c["b"] + m + 1)
                act.activation(dst[:, m, :], tmpb[:, m % 2, 0:S], ACT.Copy).then_inc(b_hi, 1)

            def rglru(i, j):
                at = START[f"b_in{i}"]
                act.preload_act_table(ACT.Gelu_apprx_tanh)
                act.wait_ge(pads_ready, DEPTH + (1 if i == 0 else 3))
                for m in range(NR):
                    split_to(at + m + 3)
                    done(at + m)
                    if m >= 2:
                        act.wait_ge(cv_ready, c["cv"] + m - 1)
                    act.activation(xpad[:, m % 2, 3:3 + S], bank(m % 6, S), ACT.Copy)
                    act.activation(cv[:, m, :], bank(m % 6, S), ACT.Identity,
                                   scale=vcol("conv_w", (j * 4 + 3) * NR + m),
                                   bias=vcol("conv_b", j * NR + m)).then_inc(b_evac, 1)
                for m in range(NR, 2 * NR):
                    split_to(at + m + 3)
                    done(at + m)
                    act.activation(gelu_g[:, m - NR, :], bank(m % 6, S), ACT.Gelu_apprx_tanh).then_inc(b_evac, 1)
                act.wait_ge(sp_step, 2)

                def decay(m):
                    act.wait_ge(gate_sig, c["cv"] + m + 1)
                    act.activation(av[:, m, :], sg[:, m % 2, 0:S], ACT.Exp,
                                   scale=n8sp[:, j * NR + m:j * NR + m + 1])
                    act.activation(th[:, m, :], sg[:, m % 2, 0:S], ACT.Tanh,
                                   scale=n8sp[:, j * NR + m:j * NR + m + 1]).then_inc(rad_ready, 1)

                for m in range(NR):
                    act.wait_ge(gate_mm, c["cv"] + m + 1)
                    if m >= 2:
                        act.wait_ge(gate_ab, c["cv"] + m - 1)
                        act.wait_ge(rad_ready, c["cv"] + m - 1)
                    act.activation(sg[:, m % 2, 0:S], ps[:, m % 4, 0:S], ACT.Exp, scale=-1.0,
                                   bias=nbx[:, j * NR + m:j * NR + m + 1])
                    act.activation(sg[:, m % 2, S:T], ps[:, m % 4, S:T], ACT.Exp, scale=-1.0,
                                   bias=nbx[:, (2 + j) * NR + m:(2 + j) * NR + m + 1]).then_inc(gate_exp, 1)
                    if m:
                        decay(m - 1)
                decay(NR - 1)
                c["cv"] += NR
                for h in range(2):
                    c["root"] += 1
                    act.wait_ge(gate_mm, c["cv"])
                    act.wait_ge(recip_done, c["rms"] + h + 1)
                    act.activation(th[:, 5 * h:5 * h + 5, :], th[:, 5 * h:5 * h + 5, :],
                                   ACT.Sqrt).then_inc(root_ready, 1)
                c["rms"] += 2
                for m in range(NR):
                    b_upper(bh, m)
                c["b"] += NR
                short_down(f"b_out{i}", NR)

            def sgu(i):
                at = START[f"b_in{i}"]
                act.preload_act_table(ACT.Gelu_apprx_tanh)
                for m in range(2 * KD):
                    split_to(at + m + 3)
                    done(at + m)
                    if m < KD:
                        act.activation(vg[:, m, :], bank(m % 6, S), ACT.Gelu_apprx_tanh).then_inc(b_evac, 1)
                        act.wait_ge(b_evac, c["bev"] + m + 1)
                        if m >= 2:
                            act.wait_ge(sq_summed, c["sq"] + m - 1)
                        act.activation(tmpa[:, m % 2, 0:S], vg[:, m, :], ACT.Square).then_inc(sq_ready, 1)
                    else:
                        act.activation(ug[:, m - KD, :], bank(m % 6, S), ACT.Gelu_apprx_tanh).then_inc(b_evac, 1)
                c["sq"] += KD
                root(S)

                def turned(m):
                    act.wait_ge(vtt_done, m + 1)
                    act.activation(vt[:, m, :], ps[:, 2 + m % 2, 0:S], ACT.Copy).then_inc(vtt_ready, 1)

                turned(0)
                for m in range(KD):
                    if m + 1 < KD:
                        turned(m + 1)
                    b_upper(bh, m)
                c["b"] += KD
                short_down(f"b_out{i}", KD)

            def conv(i):
                at = START[f"b_in{i}"]
                for m in range(KD):
                    split_to(at + 3 * m + 3)
                    done(at + 3 * m)
                    if m >= 2:
                        act.wait_ge(b_f32, c["b"] + m - 1)
                    act.activation(tmpa[:, m % 2, 0:S], bank(3 * (m % 2), S), ACT.Copy).then_inc(b_evac, 1)
                    split_to(at + 3 * m + 5)
                    b_upper(ch, m)
                c["b"] += KD
                short_down(f"b_out{i}", KD)

            for i, kind in enumerate(MIXERS):
                norm(S, dst=bh, bias=False)
                if kind == "rglru":
                    rglru(i, i // 3)
                    c["bev"] += 2 * NR
                elif kind == "sgu":
                    sgu(i)
                    c["bev"] += 2 * KD
                else:
                    conv(i)
                    c["bev"] += KD
                norm(S, dst=bh, bias=False)
                mlp_up(f"mlp_up{i}")
                down(f"mlp_down{i}", NM)
            norm(S, split_out=False)

        @block.vector
        def _(dve):
            c = Tally()

            def link(ins):
                c["chain"] += 1
                ins.then_inc(dve_chain, 1)
                dve.wait_ge(dve_chain, c["chain"])

            def split(at, dyn=0):
                if at >= N_SLOTS:
                    return
                r = at % RING
                dve.wait_ge(w_hi_ready, dyn + (at + 1))
                dve.tensor_tensor(wlo[:, r, :], raw[:, r, :], whi[:, r, :].bitcast(F32),
                                  ALU.subtract).then_inc(w_ready, 1)

            def split_to(at):
                while c["split"] <= at:
                    split(c["split"])
                    c["split"] += 1

            def done(at, dyn=0):
                dve.wait_ge(slots_done, dyn + (RING + at + 1))

            def mean_square(b, w, n):
                dve.wait_ge(sq_summed, c["sq"])
                link(dve.tensor_scalar(tmpb[:, 0, 0:w], bank(b, w), 1.0 / n, EPS, ALU.mult, ALU.add))
                dve.reciprocal(tmpb[:, 1, 0:w], tmpb[:, 0, 0:w]).then_inc(recip_done, 1)
                c["rms"] += 1

            def halves(w):
                return [slice(s * S, (s + 1) * S) for s in range(w // S)]

            def norm_mod(w, l, ord_shift, scale_at):
                c["sq"] += KD
                mean_square(0, w, D)
                c["root"] += 1
                dve.wait_ge(rstd_ready, c["root"])

                def lower(m):
                    dve.wait_ge(nh_ready, c["y"] + m + 1)
                    for s, part in enumerate(halves(w)):
                        last = dve.scalar_tensor_tensor(
                            out=nl[:, m, part], in0=tmpb[:, m % 2, part], scalar=mod[:, ord_shift, m, s:s + 1],
                            in1=nh[:, m, part].bitcast(F32), op0=ALU.add, op1=ALU.subtract)
                    last.then_inc(nl_ready, 1)

                for m in range(KD):
                    if m >= 2:
                        dve.wait_ge(nl_ready, c["y"] + m - 1)
                    for s, part in enumerate(halves(w)):
                        last = dve.scalar_tensor_tensor(
                            out=tmpb[:, m % 2, part], in0=X[:, m, part], scalar=fix[:, scale_at, m, s:s + 1],
                            in1=rstd[:, part], op0=ALU.mult, op1=ALU.mult)
                    last.then_inc(y_ready, 1)
                    if m:
                        lower(m - 1)
                lower(KD - 1)
                c["y"] += KD

            def norm_gain(gain):
                c["sq"] += KD
                mean_square(0, S, D)
                c["root"] += 1
                dve.wait_ge(rstd_ready, c["root"])

                def lower(m):
                    dve.wait_ge(nh_ready, c["y"] + m + 1)
                    dve.tensor_tensor(bl[:, m, :], tmpb[:, m % 2, 0:S], bh[:, m, :].bitcast(F32),
                                      ALU.subtract).then_inc(nl_ready, 1)

                for m in range(KD):
                    if m >= 2:
                        dve.wait_ge(nl_ready, c["y"] + m - 1)
                    dve.scalar_tensor_tensor(out=tmpb[:, m % 2, 0:S], in0=X[:, m, 0:S], scalar=vcol(*gain(m)),
                                             in1=rstd[:, 0:S], op0=ALU.mult, op1=ALU.mult).then_inc(y_ready, 1)
                    if m:
                        lower(m - 1)
                lower(KD - 1)
                c["y"] += KD

            def norm_last(name):
                c["sq"] += KD
                mean_square(0, S, D)
                c["root"] += 1
                dve.wait_ge(rstd_ready, c["root"])
                for m in range(KD):
                    dve.scalar_tensor_tensor(out=X[:, m, 0:S], in0=X[:, m, 0:S], scalar=vcol(name, m),
                                             in1=rstd[:, 0:S], op0=ALU.mult, op1=ALU.mult).then_inc(x_new, 1)

            def fix_one(l, k, g):
                n = MOD(l, g)
                dve.wait_ge(mod_ready, n + 1)
                op, val = (ALU.add, 1.0) if k < 3 else (ALU.mult, 0.5)
                link(dve.tensor_scalar(fix[:, 5 * l + k, :, :], mod[:, n, :, :], val, None, op))

            def residual(name, w, gate):
                end = START[name] + dict(PLAN)[name] - 1
                for m in range(KD):
                    if m < KD - 1:
                        dve.wait_ge(acc_done, c["acc"] + m + 1)
                    else:
                        done(end)
                    if gate is None:
                        last = dve.tensor_tensor(X[:, m, 0:S], bank(m, S), X[:, m, 0:S], ALU.add)
                    else:
                        for s, part in enumerate(halves(w)):
                            last = dve.scalar_tensor_tensor(
                                out=X[:, m, part], in0=ps[:, m, part], scalar=gate[:, m, s:s + 1],
                                in1=X[:, m, part], op0=ALU.mult, op1=ALU.add)
                    last.then_inc(x_new, 1)
                c["acc"] += KD - 1

            def unit(u, udyn, w, mlp, local, ldyn):
                dve.wait_ge(up_act, udyn + (u + 1))
                if mlp:
                    w, h, l_ = T, mh, ml
                    src = tmpa[:, u % 2, :]
                else:
                    h, l_ = hh, hl
                    src = bank(2 * (u % 2) + 1, w)
                dve.wait_ge(hid_lo, udyn + (u + 1))
                dve.tensor_tensor(tmpb[:, u % 2, 0:w], tmpa[:, u % 2, 0:w], src, ALU.mult).then_inc(up_evac, 1)
                dve.wait_ge(hid_hi, udyn + (u + 1))
                cols = bass.ds(ldyn * T + local * T, w)
                dve.tensor_tensor(l_[:, cols], tmpb[:, u % 2, 0:w], h[:, cols].bitcast(F32),
                                  ALU.subtract).then_inc(hid_lo, 1)

            def up4(at, dyn, u, udyn, w, mlp, local, ldyn):
                for q in range(2):
                    split(at + 3 + 2 * q, dyn)
                    split(at + 4 + 2 * q, dyn)
                    done(at + 2 * q + 1, dyn)
                    unit(u + q, udyn, w, mlp, local + q, ldyn)

            modf = mod[:].rearrange("p g k s -> p (g k s)")
            adabf = ada_b[:].rearrange("p g k s -> p (g k s)")

            def ada_mod(g, gdyn):
                dve.wait_ge(ada_cols_done, gdyn + (g + 1))
                cols = bass.ds(gdyn * 16 + g * 16, 16)
                dve.tensor_tensor(modf[:, cols], ps[:, 6, 0:16], adabf[:, cols], ALU.add).then_inc(mod_ready, 1)

            def ffn_up(name, w, ada_groups):
                at = START[name]
                local = 0
                if ada_groups:
                    with dve.Fori(0, ada_groups) as i:
                        for q in range(4):
                            split(at + 3 + q, i * 16)
                        up4(at + 4, i * 16, c["unit"], i * 4, w, False, 0, i * 4)
                        for q in range(4):
                            split(at + 11 + q, i * 16)
                        up4(at + 12, i * 16, c["unit"] + 2, i * 4, w, False, 2, i * 4)
                        ada_mod(c["ada"], i)
                    at += 16 * ada_groups
                    c["unit"] += 4 * ada_groups
                    c["ada"] += ada_groups
                    local = 4 * ada_groups
                left = (START[name.replace("up", "down")] - at) // 4
                with dve.Fori(0, left) as i:
                    up4(at, i * 4, c["unit"], i * 2, w, False, local, i * 2)
                c["unit"] += 2 * left
                c["split"] = at + 4 * left + 3

            def mlp_up(name):
                with dve.Fori(0, NM // 4) as i:
                    up4(START[name], i * 4, c["unit"], i * 2, S, True, 0, i * 2)
                c["unit"] += NM // 2
                c["split"] = START[name] + NM + 3

            def down(name, n_k):
                at = START[name]
                loops = n_k // 4 - 1
                with dve.Fori(0, loops) as i:
                    for q in range(4):
                        split(at + 3 + q, i * 4)
                c["split"] = at + 3 + 4 * loops
                split_to(at + n_k + 2)

            def short_down(name, n_k):
                split_to(START[name] + n_k + 2)

            def attention(l):
                units = attn_units(l)
                n = len(units)

                def normalise(u):
                    nk = len(units[u][5]) * P
                    dve.wait_ge(exp_ready, c["att"] + u + 1)
                    link(dve.reciprocal(srs[:, u:u + 1], ssm[:, u:u + 1]))
                    dve.tensor_scalar(prob[:, u % 2, 0:nk], prob[:, u % 2, 0:nk], srs[:, u:u + 1], None,
                                      ALU.mult).then_inc(prob_ready, 1)

                def o_lower(g):
                    _, s, t, *_ = units[4 * g]
                    part = slice(s * S, (s + 1) * S)
                    dve.wait_ge(o_hi, c["og"] + g + 1)
                    dve.tensor_tensor(nl[:, t, part], bank(4 + g % 2, S), nh[:, t, part].bitcast(F32),
                                      ALU.subtract).then_inc(o_lo, 1)

                for u, (g, s, t, h2, qt, kts) in enumerate(units):
                    nk = len(kts) * P
                    dve.wait_ge(s_done, c["att"] + u + 1)
                    link(dve.tensor_reduce(smx[:, u:u + 1], ps[:, u % 2, 0:nk], AX.X, ALU.max))
                    dve.tensor_scalar(snm[:, u:u + 1], smx[:, u:u + 1], -ATTN_SCALE, None,
                                      ALU.mult).then_inc(nmax_ready, 1)
                    if u:
                        normalise(u - 1)
                    if u >= 5 and u % 4 == 1:
                        o_lower(u // 4 - 1)
                normalise(n - 1)
                o_lower(n // 4 - 1)
                c["att"] += n
                c["og"] += n // 4

            def mixer1(l):
                at = START[f"in{l}"]
                w = mix_w(l)
                split_to(at + 10)
                for i in range(5):
                    a, ww = kq_at(i, w)
                    dve.wait_ge(hssq_done, 5 * l + i + 1)
                    last = dve.tensor_scalar(kqs[:, a:a + ww], bank(2 + i, ww), 1.0 / HD, EPS, ALU.mult, ALU.add)
                last.then_inc(hms_read, 1)
                dve.wait_ge(hms_read, l + 1)
                dve.reciprocal(kqs[:, 0:T + 4 * w], kqs[:, 0:T + 4 * w]).then_inc(hrecip, 1)
                split_to(at + 12)
                if l == 0:
                    at = START["ada_mid"]
                    for g in range(2):
                        split_to(at + 8 * g + 10)
                        ada_mod(c["ada"], 0)
                        c["ada"] += 1
                dve.wait_ge(hrstd, l + 1)
                for gain, cols in ((vcol("k_gain", l), slice(0, T)), (vcol("q_gain", l), slice(T, T + 4 * w))):
                    dve.scalar_tensor_tensor(out=kq[:, cols], in0=kq[:, cols], scalar=gain, in1=kqs[:, cols],
                                             op0=ALU.mult, op1=ALU.mult).then_inc(zn_ready, 1)
                for u in range(2 * (w // S)):
                    dve.wait_ge(f1_done, c["f1"] + u + 1)
                    dve.tensor_copy(ab[:, u, :, :].rearrange("p a b -> p (a b)"), bank(u % 2)).then_inc(ab_ready, 1)
                c["f1"] += 2 * (w // S)
                for s, part in enumerate(halves(w)):
                    for ch_ in range(2):
                        c["f2"] += 1
                        dve.wait_ge(f2_done, c["f2"])
                        dve.tensor_copy(yt[:, ch_, part], bank(2 + 2 * s + ch_, S)).then_inc(yt_ready, 1)
                for m in range(2):
                    dve.wait_ge(side_hi, 4 * l + m + 1)
                    dve.tensor_tensor(nl[:, 6 + m, 0:w], bank(6 + m, w), nh[:, 6 + m, 0:w].bitcast(F32),
                                      ALU.subtract).then_inc(side_lo, 1)
                for m in range(2):
                    dve.wait_ge(side_hi, 4 * l + m + 3)
                    dve.scalar_tensor_tensor(out=nl[:, 4 + m, 0:w], in0=bank(m, w),
                                             scalar=vcol("pool_scale", 2 * l + m),
                                             in1=nh[:, 4 + m, 0:w].bitcast(F32), op0=ALU.mult,
                                             op1=ALU.subtract).then_inc(side_lo, 1)
                dve.wait_ge(zn_ready, 2 * (l + 1))
                for i in range(5):
                    a, _ = kq_at(i, w)
                    dve.wait_ge(rot_done, 5 * l + i + 1)
                    dve.tensor_tensor(rot[:, i % 2, :], bank(2 + i, S), ccol("sin", 0, S), ALU.mult)
                    link(dve.tensor_tensor(kq[:, a:a + S], kq[:, a:a + S], ccol("cos", 0, S), ALU.mult))
                    dve.tensor_tensor(kq[:, a:a + S], kq[:, a:a + S], rot[:, i % 2, :], ALU.add).then_inc(qk_ready, 1)
                attention(l)
                short_down(f"out{l}", KD)

            dve.sem_inc(up_evac, 2)
            dve.sem_inc(hid_lo, 2)
            dve.wait_ge(c_hi_ready, 1)
            view = cst4[:, 0:32].rearrange("p (k c) -> p k c", c=4)
            dve.tensor_tensor(view[:, :, 2:4], csil[:], view[:, :, 0:2].bitcast(F32),
                              ALU.subtract).then_inc(c_ready, 1)
            for g in range(2):
                split_to(8 * g + 10)
                ada_mod(g, 0)
                c["ada"] += 1
            dve.wait_ge(x_loaded, 16)
            dve.sem_inc(x_new, KD)
            for l in range(DEPTH):
                fix_one(l, 0, 1)
                norm_mod(T, l, MOD(l, 0), 5 * l)
                ffn_up(f"ffn1_up{l}", T, 5 if l == 0 else 4)
                down(f"ffn1_down{l}", NF)
                fix_one(l, 3, 2)
                fix_one(l, 1, 4)
                residual(f"ffn1_down{l}", T, fix[:, 5 * l + 3, :, :])
                norm_mod(T, l, MOD(l, 3), 5 * l + 1)
                mixer1(l)
                w = mix_w(l)
                fix_one(l, 2, 7)
                fix_one(l, 4, 8)
                dve.wait_ge(mod_ready, MOD(l, 5) + 1)
                residual(f"out{l}", w, mod[:, MOD(l, 5), :, :])
                norm_mod(w, l, MOD(l, 6), 5 * l + 2)
                ffn_up(f"ffn2_up{l}", w, 5 if l == 0 else 0)
                down(f"ffn2_down{l}", NF)
                residual(f"ffn2_down{l}", w, fix[:, 5 * l + 4, :, :])
            norm_last("final1")
            e, d_, r_, z, z2 = (sp_t[:, k, :] for k in range(1, 6))
            lam = vec[:, VEC["lam"]:VEC["lam"] + 2 * NR]
            dve.wait_ge(sp_step, 1)
            link(dve.tensor_scalar(d_, e, 2.0, None, ALU.add))
            link(dve.reciprocal(r_, d_))
            link(dve.tensor_tensor(z, e, r_, ALU.mult))
            link(dve.tensor_tensor(z2, z, z, ALU.mult))
            link(dve.tensor_scalar(d_, z2, 1.0 / 17, None, ALU.mult))
            for k in (15, 13, 11, 9, 7, 5, 3):
                link(dve.scalar_tensor_tensor(out=d_, in0=d_, scalar=1.0 / k, in1=z2, op0=ALU.add, op1=ALU.mult))
            link(dve.scalar_tensor_tensor(out=d_, in0=d_, scalar=1.0, in1=z, op0=ALU.add, op1=ALU.mult))
            link(dve.tensor_scalar(r_, lam, -1.0, 0.0, ALU.mult, ALU.max))
            link(dve.scalar_tensor_tensor(out=d_, in0=d_, scalar=2.0, in1=r_, op0=ALU.mult, op1=ALU.add))
            dve.tensor_scalar(n8sp[:], d_, -8.0, None, ALU.mult)
            dve.tensor_scalar(nbx[:], vec[:, VEC["ba"]:VEC["ba"] + 4 * NR], -1.0, None,
                              ALU.mult).then_inc(sp_step, 1)

            def b_lower(h, l_, m):
                dve.wait_ge(b_hi, c["b"] + m + 1)
                dve.tensor_tensor(l_[:, m, :], tmpb[:, m % 2, 0:S], h[:, m, :].bitcast(F32),
                                  ALU.subtract).then_inc(b_lo, 1)

            def rglru(i, j):
                at = START[f"b_in{i}"]
                for m in range(NR):
                    split_to(at + m + 3)
                    dve.wait_ge(b_evac, c["bev"] + m + 1)
                    for tap in range(3):
                        ins = dve.scalar_tensor_tensor(
                            out=cv[:, m, :], in0=xpad[:, m % 2, tap:tap + S],
                            scalar=vcol("conv_w", (j * 4 + tap) * NR + m), in1=cv[:, m, :],
                            op0=ALU.mult, op1=ALU.add)
                        if tap < 2:
                            link(ins)
                    ins.then_inc(cv_ready, 1)
                split_to(at + 2 * NR + 2)
                for h in range(2):
                    for m in range(5 * h, 5 * h + 5):
                        dve.wait_ge(gate_exp, c["cv"] + m + 1)
                        link(dve.tensor_scalar(sg[:, m % 2, :], sg[:, m % 2, :], 1.0, None, ALU.add))
                        dve.reciprocal(sg[:, m % 2, :], sg[:, m % 2, :]).then_inc(gate_sig, 1)
                        dve.wait_ge(gate_sig, c["cv"] + m + 1)
                        dve.tensor_tensor(ix[:, m, :], sg[:, m % 2, S:T], cv[:, m, :], ALU.mult).then_inc(gate_ab, 1)
                    half = slice(5 * h, 5 * h + 5)
                    dve.wait_ge(rad_ready, c["cv"] + 5 * h + 5)
                    link(dve.tensor_scalar(dd[:, half, :], th[:, half, :], -1.0, 1.0, ALU.mult, ALU.add))
                    link(dve.reciprocal(dd[:, half, :], dd[:, half, :]))
                    dve.scalar_tensor_tensor(out=th[:, half, :], in0=th[:, half, :], scalar=-2.0,
                                             in1=dd[:, half, :], op0=ALU.mult, op1=ALU.mult).then_inc(recip_done, 1)
                for h in range(2):
                    half = slice(5 * h, 5 * h + 5)
                    c["root_b"] += 1
                    dve.wait_ge(root_ready, c["root_b"])
                    dve.wait_ge(gate_ab, c["cv"] + NR)
                    link(dve.tensor_tensor(ix[:, half, :], ix[:, half, :], th[:, half, :], ALU.mult))
                    for m in range(5 * h, 5 * h + 5):
                        link(dve.tensor_tensor_scan(dd[:, m, :], av[:, m, :], ix[:, m, :], 0.0, ALU.mult, ALU.add))
                        if m >= 2:
                            dve.wait_ge(b_lo, c["b"] + m - 1)
                        dve.tensor_tensor(tmpb[:, m % 2, 0:S], dd[:, m, :], gelu_g[:, m, :],
                                          ALU.mult).then_inc(b_f32, 1)
                        if m:
                            b_lower(bh, bl, m - 1)
                b_lower(bh, bl, NR - 1)
                c["cv"] += NR
                c["b"] += NR
                c["bev"] += 2 * NR
                short_down(f"b_out{i}", NR)

            def sgu(i):
                at = START[f"b_in{i}"]
                split_to(at + 2 * KD + 2)
                c["sq"] += KD
                mean_square(7, S, D)
                c["root"] += 1
                dve.wait_ge(rstd_ready, c["root"])

                def scaled(m):
                    if m >= 2:
                        dve.wait_ge(vtt_done, m - 1)
                    dve.scalar_tensor_tensor(out=vn[:, m % 2, :], in0=vg[:, m, :], scalar=vcol("b_norm", m),
                                             in1=rstd[:, 0:S], op0=ALU.mult, op1=ALU.mult).then_inc(vn_ready, 1)

                scaled(0)
                for m in range(KD):
                    if m + 1 < KD:
                        scaled(m + 1)
                    dve.wait_ge(mixd_done, m + 1)
                    if m >= 2:
                        dve.wait_ge(b_lo, c["b"] + m - 1)
                    dve.tensor_tensor(tmpb[:, m % 2, 0:S], bank(m % 2, S), ug[:, m, :], ALU.mult).then_inc(b_f32, 1)
                    b_lower(bh, bl, m)
                c["b"] += KD
                c["bev"] += 2 * KD
                short_down(f"b_out{i}", KD)

            def conv(i):
                at = START[f"b_in{i}"]
                dve.wait_ge(pads_ready, DEPTH + 2)
                for m in range(KD):
                    split_to(at + 3 * m + 5)
                    dve.wait_ge(b_evac, c["bev"] + m + 1)
                    done(at + 3 * m + 1)
                    acc = tmpb[:, m % 2, 0:S]
                    b = 3 * (m % 2)
                    link(dve.tensor_tensor(cpad[:, m % 2, 2:2 + S], tmpa[:, m % 2, 0:S], bank(b + 1, S), ALU.mult))
                    link(dve.tensor_scalar(acc, cpad[:, m % 2, 0:S], vcol("c_conv", m), None, ALU.mult))
                    for tap in (1, 2):
                        link(dve.scalar_tensor_tensor(out=acc, in0=cpad[:, m % 2, tap:tap + S],
                                                      scalar=vcol("c_conv", tap * KD + m), in1=acc,
                                                      op0=ALU.mult, op1=ALU.add))
                    done(at + 3 * m + 2)
                    dve.tensor_tensor(acc, acc, bank(b + 2, S), ALU.mult).then_inc(b_f32, 1)
                    b_lower(ch, cl, m)
                c["b"] += KD
                c["bev"] += KD
                short_down(f"b_out{i}", KD)

            for i, kind in enumerate(MIXERS):
                norm_gain(lambda m, i=i: ("norm_mix", i * KD + m))
                if kind == "rglru":
                    rglru(i, i // 3)
                elif kind == "sgu":
                    sgu(i)
                else:
                    conv(i)
                residual(f"b_out{i}", S, None)
                norm_gain(lambda m, i=i: ("norm_mlp", i * KD + m))
                mlp_up(f"mlp_up{i}")
                down(f"mlp_down{i}", NM)
                residual(f"mlp_down{i}", S, None)
            norm_last("final2")

        @block.gpsimd
        def _(pool):
            c = Tally()

            def link(ins):
                c["chain"] += 1
                ins.then_inc(pool_chain, 1)
                pool.wait_ge(pool_chain, c["chain"])

            pool.memset(ones[:], 1.0)
            pool.memset(cst4[:].bitcast(F32), 0.0).then_inc(consts_ready, 1)
            for l in range(DEPTH):
                w = mix_w(l)
                seg = w // S
                pool.wait_ge(slots_done, RING + START[f"in{l}"])
                pool.dma_start(cst[:], cst_in).then_inc(mix_loaded, 16)
                pool.dma_start(fftw[:], fftw_in[l]).then_inc(mix_loaded, 16)
                pool.dma_start(poolw[:], poolw_in[l]).then_inc(mix_loaded, 16)
                pool.memset(up[:], 0.0).then_inc(pads_ready, 1)
                pool.wait_ge(z_ready, 10 * l + 8)
                u = up[:, :, 0:seg, :]
                link(pool.tensor_tensor(w2[:, :, 0:seg, 1:PADW], u[:, :, :, 0:PADW - 1], u[:, :, :, 1:PADW],
                                        ALU.add))
                link(pool.tensor_tensor(w4[:, :, 0:seg, 2:PADW - 1], w2[:, :, 0:seg, 1:PADW - 2],
                                        w2[:, :, 0:seg, 3:PADW], ALU.add))
                link(pool.tensor_tensor(w8[:, 0:seg, 4:PADW - 3], w4[:, 1, 0:seg, 2:PADW - 5],
                                        w4[:, 1, 0:seg, 6:PADW - 1], ALU.add))
                link(pool.tensor_tensor(w16[:, 0:seg, 8:8 + S], w8[:, 0:seg, 4:4 + S], w8[:, 0:seg, 12:12 + S],
                                        ALU.add))
                pool.wait_ge(mix_loaded, 48 * (l + 1))
                cnt = cst[:, CST["inv_cnt"]:CST["inv_cnt"] + 2 * S].rearrange("p (a t) -> p a t", a=2)
                lo, hi = slice(0, 64), slice(64, 128)
                for s in range(seg):
                    for rows, tile, sums in ((lo, 0, w2[lo, 0, s, 8:8 + S]), (hi, 0, w4[hi, 0, s, 8:8 + S]),
                                             (lo, 1, w8[lo, s, 8:8 + S]), (hi, 1, w16[hi, s, 8:8 + S])):
                        last = pool.tensor_tensor(pc[rows, tile, s, :], sums, cnt[rows, tile, :], ALU.mult)
                link(last)
                pool.tensor_tensor(pc[:, :, 0:seg, :], pc[:, :, 0:seg, :], up[:, :, 0:seg, 8:8 + S],
                                   ALU.subtract).then_inc(pool_ready, 1)
            for i, kind in enumerate(MIXERS):
                pool.wait_ge(x_new, (2 + 3 * DEPTH + 2 * i) * KD)
                if kind == "rglru":
                    pool.dma_start(gates_w[:], gate_in[i // 3]).then_inc(small_loaded, 16)
                    pool.memset(xpad[:, :, 0:3], 0.0).then_inc(pads_ready, 1)
                elif kind == "sgu":
                    pool.dma_start(sbias[:], sb_in).then_inc(small_loaded, 16)
                    pool.dma_start(ws[:], ws_in).then_inc(small_loaded, 16)
                    pool.wait_ge(small_loaded, SMALL[i])
                    pool.affine_select(out=ws[:], in_=ws[:], compare_op=ALU.is_ge, fill=0.0, base=0,
                                       pattern=[[0, KD], [1, P]], channel_multiplier=-1).then_inc(ws_ready, 1)
                else:
                    pool.memset(cpad[:, :, 0:2], 0.0).then_inc(pads_ready, 1)


def MOD(l, g):
    return ADA_ORDER.index((l, g))


def up_slots(w, kd=KD):
    m = w.shape[1] // P
    return w.reshape(kd, P, m, P).transpose(2, 1, 0, 3).reshape(m, P, kd * P)


def down_slots(w):
    return w.reshape(w.shape[0] // P, P, SLOT)


def ada_slots(w, g):
    return w[:, g * SLOT:(g + 1) * SLOT].reshape(KD, P, SLOT)


def columns(v):
    return v.reshape(-1, P).T


def tables():
    f4 = np.float32
    t = np.arange(S)
    inv = (f4(10000.0) ** (-np.arange(HD // 4, dtype=f4) / f4(HD // 4))).astype(f4)
    row, col = (t // GRID_W).astype(f4), (t % GRID_W).astype(f4)
    ang = np.concatenate([row[:, None] * inv, col[:, None] * inv], axis=-1).astype(f4)
    which = np.arange(P) % (HD // 2)
    cst = np.zeros((P, N_CST), f4)

    def put(name, a):
        cst[:, CST[name]:CST[name] + a.shape[1]] = a

    put("cos", np.cos(ang).T[which])
    put("sin", np.sin(ang).T[which])
    ch = np.arange(HD)
    wc = 2 * np.pi * np.outer(ch, ch) / HD
    eye = np.eye(2)
    put("dft_c", np.concatenate([np.kron(eye, np.cos(wc)), np.kron(eye, np.sin(wc))], axis=1))
    wt = 2 * np.pi * (np.outer(t, t) % S) / S
    norm = 1.0 / np.sqrt(S * HD)
    cs = np.stack([np.cos(wt), -np.sin(wt)]) * norm
    put("dft_s", cs.reshape(2, 2, P, S).transpose(2, 1, 0, 3).reshape(P, 4 * S))
    cnt = np.zeros((2, P, S))
    for g, w in enumerate((2, 4, 8, 16)):
        n = np.clip(t + w - w // 2, 0, S) - np.clip(t - w // 2, 0, S)
        cnt[g // 2, 64 * (g % 2):64 * (g % 2) + 64] = 1.0 / n
    put("inv_cnt", cnt.transpose(1, 0, 2).reshape(P, 2 * S))
    swap = np.zeros((P, P))
    for m in range(P):
        if m % HD < HD // 2:
            swap[m + HD // 2, m] = -1.0
        else:
            swap[m - HD // 2, m] = 1.0
    put("swap", swap)
    put("blk", np.kron(eye, np.ones((HD, HD))))
    small = np.zeros((P, 2 + P), f4)
    small[0, 0] = small[2, 0] = small[1, 1] = small[3, 1] = 1.0
    small[:, 2:] = np.eye(P)
    return cst, small


def kernel(**inputs):
    import concourse.bacc as bacc
    from concourse.bass_utils import run_bass_kernel_spmd

    v = {k: np.asarray(a) for k, a in inputs.items()}
    stream = np.empty((N_SLOTS, P, SLOT), np.float32)

    def put(name, a, skip=0):
        stream[START[name] + skip:START[name] + skip + len(a)] = a

    heads = [h for t in range(4) for h in (t, t + 4)]
    order = np.concatenate([np.arange(h * HD, (h + 1) * HD) for h in heads])
    aw = 8 * HD
    in_cols = np.concatenate([np.arange(aw, aw + 2 * P), order, np.arange(aw + 2 * P, aw + 6 * P)])

    def ffn_up(name, w, groups):
        half = w.shape[1] // 2
        g, u = up_slots(w[:, :half]), up_slots(w[:, half:])
        slots = np.stack([g, u], axis=1).reshape(2 * NF, P, SLOT)
        at = 0
        for n, (l, grp) in enumerate(groups):
            a = ada_slots(v["ada_w"][l], grp)
            put(name, np.concatenate([a[:4], slots[8 * n:8 * n + 4], a[4:], slots[8 * n + 4:8 * n + 8]]), 16 * n)
            at = 8 * (n + 1)
        put(name, slots[at:], 16 * len(groups))

    put("ada_head", np.concatenate([ada_slots(v["ada_w"][0], g) for g in (0, 1)]))
    put("ada_mid", np.concatenate([ada_slots(v["ada_w"][0], g) for g in (7, 8)]))
    for l in range(DEPTH):
        ffn_up(f"ffn1_up{l}", v["ffn1_w_gu"][l], ADA_ORDER[2:7] if l == 0 else ADA_ORDER[14:18])
        put(f"ffn1_down{l}", down_slots(v["ffn1_w_down"][l]))
        put(f"in{l}", up_slots(v["w_in"][l][:, in_cols]))
        w = v["w_out"][l]
        w = down_slots(np.concatenate([w[order], w[aw:]]))
        put(f"out{l}", w[[4, 5, 6, 7, 0, 1, 2, 3]])
        ffn_up(f"ffn2_up{l}", v["ffn2_w_gu"][l], ADA_ORDER[9:14] if l == 0 else [])
        put(f"ffn2_down{l}", down_slots(v["ffn2_w_down"][l]))
    for i, kind in enumerate(MIXERS):
        if kind == "rglru":
            w = up_slots(v["a_w_in_2"][i // 3])
            put(f"b_in{i}", np.concatenate([w[NR:], w[:NR]]))
            put(f"b_out{i}", down_slots(v["a_w_out_2"][i // 3]))
        elif kind == "sgu":
            w = up_slots(v["b_w_in_2"][0])
            put(f"b_in{i}", np.concatenate([w[KD:], w[:KD]]))
            put(f"b_out{i}", down_slots(v["b_w_out_2"][0]))
        else:
            w = up_slots(v["c_w_in_2"][0]).reshape(3, KD, P, SLOT)
            put(f"b_in{i}", w[[1, 2, 0]].transpose(1, 0, 2, 3).reshape(3 * KD, P, SLOT))
            put(f"b_out{i}", down_slots(v["c_w_out_2"][0]))
        put(f"mlp_up{i}", up_slots(v["mlp_w1_2"][i]))
        put(f"mlp_down{i}", down_slots(v["mlp_w2_2"][i]))

    vec = np.zeros((P, N_VEC), np.float32)

    def vput(name, a):
        vec[:, VEC[name]:VEC[name] + a.shape[1]] = a

    for name, key in [("final1", "final_gain"), ("final2", "final_norm_g_2"), ("norm_mix", "norm_mix_g_2"),
                      ("norm_mlp", "norm_mlp_g_2"), ("conv_w", "a_conv_w_2"), ("conv_b", "a_conv_b_2"),
                      ("ba", "a_gate_a_b_2"), ("bx", "a_gate_x_b_2"), ("lam", "a_lambda_2"),
                      ("b_norm", "b_norm_g_2"), ("c_conv", "c_conv_w_2"), ("pool_scale", "pool_scale")]:
        vput(name, columns(v[key]))
    vput("q_gain", np.concatenate([v["q_gain"], v["q_gain"]], axis=1).T)
    vput("k_gain", np.concatenate([v["k_gain"], v["k_gain"]], axis=1).T)

    ada_b = np.stack([v["ada_b"][l, g * D:(g + 1) * D].reshape(KD, P).T for l, g in ADA_ORDER], axis=1)
    poolw = np.zeros((DEPTH, P, 2, P), np.float32)
    for g in range(4):
        o = 64 * (g % 2)
        poolw[:, o:o + 64, g // 2, o:o + 64] = v["pool_w"][:, g]
    gates = np.zeros((2, P, 2, NR, 3 * P), np.float32)
    for g, key in enumerate(("a_gate_a_w_2", "a_gate_x_w_2")):
        for h in range(D_RNN // A_HD):
            for r0 in range(h * A_HD, (h + 1) * A_HD):
                k = r0 // P
                o = h * A_HD - (k - 1) * P
                gates[:, r0 % P, g, k, o:o + A_HD] = v[key][:, h, r0 - h * A_HD]
    x = np.zeros((P, KD, T), np.float32)
    x[:, :, :S] = v["x"][0].T.reshape(KD, P, S).transpose(1, 0, 2)
    x[:, :, S:] = v["ctx"][0].T.reshape(KD, P, S).transpose(1, 0, 2)
    cst, small = tables()
    arrays = {
        "x_in": x,
        "stream": stream,
        "vec_in": vec,
        "cvec_in": np.stack([v["c"][0].reshape(KD, P).T, v["c_ctx"].reshape(KD, P).T], axis=2),
        "ada_b_in": np.stack([ada_b, ada_b], axis=3),
        "cst_in": cst,
        "small_in": small,
        "fftw_in": v["fft_w"].reshape(DEPTH, 2, P, 2 * P).transpose(0, 2, 1, 3),
        "poolw_in": poolw,
        "gate_in": gates,
        "ws_in": v["b_w_s_2"][0].transpose(2, 0, 1),
        "sb_in": v["b_s_bias_2"][0].reshape(1, KD * P),
    }
    nc = bacc.Bacc("TRN2", target_bir_lowering=False, num_devices=1)
    arrays = {k: np.ascontiguousarray(a) for k, a in arrays.items()}
    args = [nc.dram_tensor(k, a.shape, mybir.dt.from_np(a.dtype), kind="ExternalInput").ap()
            for k, a in arrays.items()]
    out = nc.dram_tensor("out", (P, KD, S), F32, kind="ExternalOutput").ap()
    build(nc, *args, out)
    r = run_bass_kernel_spmd(nc, [arrays], core_ids=[0])
    got = np.asarray(r.results[0]["out"])
    return np.ascontiguousarray(got.transpose(2, 1, 0).reshape(1, S, D))
```

```python
from contextlib import ExitStack

import numpy as np

import concourse.bass as bass
from concourse import mybir

F32 = mybir.dt.float32
F32R = mybir.dt.float32r
ACT = mybir.ActivationFunctionType
ALU = mybir.AluOpType
AX = mybir.AxisListType

P = 128
D = 1024
KD = D // P
S = 256
T = 2 * S
DEPTH = 2
N_MOD = 9
D_FF = 2816
NF = D_FF // P
D_MLP = 4096
NM = D_MLP // P
IN_TILES = 10
HD = 64
D_RNN = 1280
NR = D_RNN // P
A_HD = 80
EPS = 1e-6
ATTN_SCALE = HD ** -0.5
GRID_W = 64
RING = 4
SLOT = 1024
PADW = 272

PLAN = [("ada_head", 16)]
for _l in range(DEPTH):
    PLAN.append((f"ffn1_up{_l}", 2 * NF + (40 if _l == 0 else 32)))
    PLAN.append((f"ffn1_down{_l}", NF))
    PLAN.append((f"in{_l}", IN_TILES + (16 if _l == 0 else 0)))
    PLAN.append((f"out{_l}", KD))
    PLAN.append((f"ffn2_up{_l}", 2 * NF + (40 if _l == 0 else 0)))
    PLAN.append((f"ffn2_down{_l}", NF))
MIXERS = ["rglru", "sgu", "conv", "rglru"]
UP2 = {"rglru": 2 * NR, "sgu": 2 * KD, "conv": 3 * KD}
DOWN2 = {"rglru": NR, "sgu": KD, "conv": KD}
for _i, _kind in enumerate(MIXERS):
    PLAN += [(f"b_in{_i}", UP2[_kind]), (f"b_out{_i}", DOWN2[_kind]),
             (f"mlp_up{_i}", NM), (f"mlp_down{_i}", NM)]
START = {}
_n = 0
for _name, _k in PLAN:
    START[_name] = _n
    _n += _k
N_SLOTS = _n
assert N_SLOTS % RING == 0

LAST_EPOCH = 1 + 3 * DEPTH + 1 + 2 * len(MIXERS)

ADA_ORDER = ([(0, 0), (0, 1)] + [(0, g) for g in range(2, 7)] + [(0, 7), (0, 8)]
             + [(1, g) for g in range(9)])

NORMS = 3 * DEPTH + 2
NORM_SQ = (NORMS - 1) * KD

HEAD_G = 4
RNN_TAIL = [(), (), (0,), (1,), (2,), (3,)]

SGU_TURN = [(), (0, 1), (2, 3), (4,), (5,), (6,), (7,), ()]
SGU_MIX = [(), (), (0, 1), (2,), (3,), (4,), (5, 6), (7,)]
SGU_GATED = [(), (), (0, 1), (2,), (3,), (4,), (5,), (6, 7)]

ADA_GROUP = [("gate", 0), ("up", 0), ("ada", 0), ("ada", 1), ("gate", 1), ("up", 1), ("ada", 2), ("ada", 3),
             ("gate", 2), ("up", 2), ("ada", 4), ("ada", 5), ("ada", 6), ("gate", 3), ("ada", 7), ("up", 3)]

GATE_K = {m: [k for k in range(max(0, m - 1), min(NR, m + 2))
              if any(h * A_HD < (k + 1) * P and (h + 1) * A_HD > k * P
                     and h * A_HD < (m + 1) * P and (h + 1) * A_HD > m * P
                     for h in range(D_RNN // A_HD))] for m in range(NR)}
GATE_BLOCKS = [(k, m) for m in range(NR) for k in GATE_K[m]]

VEC = {}
_n = 0
for _name, _k in [("final1", KD), ("final2", KD), ("norm_mix", 4 * KD), ("norm_mlp", 4 * KD),
                  ("conv_w", 2 * 4 * NR), ("conv_b", 2 * NR), ("ba", 2 * NR), ("bx", 2 * NR),
                  ("lam", 2 * NR), ("b_norm", KD), ("c_conv", 3 * KD),
                  ("q_gain", DEPTH), ("k_gain", DEPTH), ("pool_scale", 2 * DEPTH)]:
    VEC[_name] = _n
    _n += _k
N_VEC = _n

CST = {}
_n = 0
for _name, _k in [("cos", S), ("sin", S), ("dft_c", 2 * P), ("dft_s", 4 * S), ("inv_cnt", 2 * S),
                  ("swap", P), ("blk", P)]:
    CST[_name] = _n
    _n += _k
N_CST = _n


class Tally(dict):

    def __missing__(self, key):
        return 0


def build(nc, x_in, stream, vec_in, cvec_in, ada_b_in, cst_in, ident_in, fftw_in, poolw_in,
          gate_in, ws_in, sb_in, out):
    with ExitStack() as ctx:
        def sem(name):
            return ctx.enter_context(nc.semaphore(name))

        place = [nc.sbuf_base]

        def sb(name, shape, dt=F32):
            size = 4 * int(np.prod(shape[1:]))
            off = (place[0] + 31) // 32 * 32
            place[0] = off + size
            assert place[0] <= nc.sbuf_usable_end, (name, place[0])
            return nc.alloc_sbuf_tensor_at(name, shape, dt, offset=off)

        X = sb("X", [P, KD, T])
        raw = sb("raw", [P, RING, SLOT])
        whi = sb("whi", [P, RING, SLOT], F32R)
        wlo = sb("wlo", [P, RING, SLOT], F32R)
        tmpa = sb("tmpa", [P, 2, T])
        tmpb = sb("tmpb", [P, 2, T])
        ones = sb("ones", [P, P])
        ident = sb("ident", [P, P])
        sqsum = sb("sqsum", [P, T])
        tok_inv = sb("tok_inv", [P, 8])
        tok_rstd = sb("tok_rstd", [P, 4])
        vec = sb("vec", [P, N_VEC])
        n4sp = sb("n4sp", [P, 2 * NR])
        sp_t = sb("sp_t", [P, 6, 2 * NR])
        common = place[0]
        nh = sb("nh", [P, KD, T], F32R)
        nl = sb("nl", [P, KD, T], F32R)
        cst4 = sb("cst4", [P, 8 * 4 + 124], F32R)
        csil = sb("csil", [P, KD, 2])
        cvec = sb("cvec", [P, KD, 2])
        ada_row = sb("ada_row", [4, SLOT])
        mod = sb("mod", [P, DEPTH * N_MOD, KD, 2])
        ada_b = sb("ada_b", [P, DEPTH * N_MOD, KD, 2])
        fix = sb("fix", [P, DEPTH * 5, KD, 2])
        mixer = place[0]
        hh = sb("hh", [P, NF * T], F32R)
        hl = sb("hl", [P, NF * T], F32R)
        hidden_s_end = mixer + 8 * NF * S
        place[0] = mixer
        cst = sb("cst", [P, N_CST])
        fftw = sb("fftw", [P, 2, 2 * P])
        poolw = sb("poolw", [P, 2, P])
        kq = sb("kq", [P, T + 4 * T])
        kqs = sb("kqs", [P, T + 4 * T])
        qinv = sb("qinv", [P, 2, 32])
        qscale = sb("qscale", [P, 2, 32])
        zv = sb("zv", [P, T])
        zf = sb("zf", [P, 2, T])
        vtok = sb("vtok", [P, 4, P])
        rot = sb("rot", [P, 2, S])
        up = sb("up", [P, 2, 2, PADW])
        pc = sb("pc", [P, 2, 2, S])
        yt = sb("yt", [P, 2, T])
        ab = sb("ab", [P, 4, 2, 2 * P])
        smx = sb("smx", [P, 32])
        snm = sb("snm", [P, 32])
        ssm = sb("ssm", [P, 32])
        srs = sb("srs", [P, 32])
        scratch = place[0]
        w2 = sb("w2", [P, 2, 2, PADW])
        w4 = sb("w4", [P, 2, 2, PADW])
        w8 = sb("w8", [P, 2, PADW])
        w16 = sb("w16", [P, 2, PADW])
        place[0] = scratch
        prob = sb("prob", [P, 4, T])
        probT = sb("probT", [P, 2, 4, S])
        assert place[0] <= mixer + 8 * NF * T
        place[0] = common
        bh = sb("bh", [P, KD, S], F32R)
        bl = sb("bl", [P, KD, S], F32R)
        oh = sb("oh", [P, NR, S], F32R)
        ol = sb("ol", [P, NR, S], F32R)
        inv_row = sb("inv_row", [P, T])
        rstd_row = sb("rstd_row", [P, S])
        second = place[0]
        mh = sb("mh", [P, NM * S], F32R)
        ml = sb("ml", [P, NM * S], F32R)
        gates_at = (nc.sbuf_usable_end - 4 * 2 * len(GATE_BLOCKS) * P) // 32 * 32
        assert place[0] <= gates_at and hidden_s_end <= gates_at
        place[0] = gates_at
        gates_w = sb("gates_w", [P, 2, len(GATE_BLOCKS), P])
        place[0] = second
        gelu_g = sb("gelu_g", [P, NR, S])
        xpad = sb("xpad", [P, 2, 3 + S])
        cv = sb("cv", [P, NR, S])
        sg = sb("sg", [P, 2, 2 * S])
        av = sb("av", [P, NR, S])
        th = sb("th", [P, NR, S])
        ix = sb("ix", [P, NR, S])
        dd = sb("dd", [P, 3, S])
        hs = sb("hs", [P, 2, S])
        assert place[0] <= gates_at
        place[0] = second
        ws = sb("ws", [P, KD, P])
        sbias = sb("sbias", [1, KD * P])
        vg = sb("vg", [P, KD, S])
        ug = sb("ug", [P, KD, S])
        vsq = sb("vsq", [P, 2, S])
        zrow = sb("zrow", [P, 2, S])
        vt = sb("vt", [P, KD, S])
        place[0] = second
        cpad = sb("cpad", [P, 2, 2 + S])
        gcr = sb("gcr", [P, 2, S])

        ps = ctx.enter_context(nc.psum_tensor("ps", [P, 8, T], F32))

        x_loaded = sem("x_loaded")
        vec_loaded = sem("vec_loaded")
        cond_loaded = sem("cond_loaded")
        mix_loaded = sem("mix_loaded")
        raw_loaded = [sem(f"raw_loaded{r}") for r in range(RING)]
        w_hi_ready = sem("w_hi_ready")
        w_ready = sem("w_ready")
        slots_done = sem("slots_done")
        acc_done = sem("acc_done")
        x_new = sem("x_new")
        sq_ready = sem("sq_ready")
        sq_summed = sem("sq_summed")
        recip_done = sem("recip_done")
        rstd_ready = sem("rstd_ready")
        rows_ready = sem("rows_ready")
        part_added = sem("part_added")
        all_added = sem("all_added")
        sq_added = sem("sq_added")
        col_sums = sem("col_sums")
        inv_spread = sem("inv_spread")
        row_copied = sem("row_copied")
        relu_scaled = sem("relu_scaled")
        y_ready = sem("y_ready")
        nh_ready = sem("nh_ready")
        nl_ready = sem("nl_ready")
        up_act = sem("up_act")
        up_evac = sem("up_evac")
        hid_hi = sem("hid_hi")
        hid_lo = sem("hid_lo")
        csil_ready = sem("csil_ready")
        c_hi_ready = sem("c_hi_ready")
        c_ready = sem("c_ready")
        ada_row_ready = sem("ada_row_ready")
        ada_cols_done = sem("ada_cols_done")
        mod_begun = sem("mod_begun")
        mod_ready = sem("mod_ready")
        dve_chain = sem("dve_chain")
        act_chain = sem("act_chain")
        pool_chain = sem("pool_chain")
        consts_ready = sem("consts_ready")
        pads_ready = sem("pads_ready")
        z_ready = sem("z_ready")
        hssq_done = sem("hssq_done")
        hms_read = sem("hms_read")
        hrecip = sem("hrecip")
        hrstd = sem("hrstd")
        zn_ready = sem("zn_ready")
        rot_done = sem("rot_done")
        qk_ready = sem("qk_ready")
        vt_done = sem("vt_done")
        vtok_ready = sem("vtok_ready")
        f1_done = sem("f1_done")
        ab_ready = sem("ab_ready")
        f2_done = sem("f2_done")
        yt_ready = sem("yt_ready")
        pool_ready = sem("pool_ready")
        side_done = sem("side_done")
        side_hi = sem("side_hi")
        side_lo = sem("side_lo")
        s_done = sem("s_done")
        nmax_ready = sem("nmax_ready")
        exp_ready = sem("exp_ready")
        prob_ready = sem("prob_ready")
        pt_done = sem("pt_done")
        pts_ready = sem("pts_ready")
        o_done = sem("o_done")
        o_hi = sem("o_hi")
        o_lo = sem("o_lo")
        sp_step = sem("sp_step")
        b_evac = sem("b_evac")
        b_f32 = sem("b_f32")
        b_hi = sem("b_hi")
        b_lo = sem("b_lo")
        cv_ready = sem("cv_ready")
        cv_begun = sem("cv_begun")
        gelu_ready = sem("gelu_ready")
        gate_ready = sem("gate_ready")
        th_ready = sem("th_ready")
        av_ready = sem("av_ready")
        ix_ready = sem("ix_ready")
        gate_mm = sem("gate_mm")
        root_ready = sem("root_ready")
        small_loaded = sem("small_loaded")
        gates_loaded = sem("gates_loaded")
        ws_ready = sem("ws_ready")
        vsq_ready = sem("vsq_ready")
        v_added = sem("v_added")
        vg_scaled = sem("vg_scaled")
        vtt_done = sem("vtt_done")
        vtt_ready = sem("vtt_ready")
        mixd_done = sem("mixd_done")
        out_sem = sem("out_sem")

        def vcol(name, i):
            return vec[:, VEC[name] + i:VEC[name] + i + 1]

        def ccol(name, a, b):
            return cst[:, CST[name] + a:CST[name] + b]

        def norm_buf(m):
            return (tmpa, tmpb)[m // 2 % 2][:, m % 2, :]

        def square_buf(m):
            return tmpa[:, m // 2 % 2, m % 2 * S:(m % 2 + 1) * S]

        def bank(b, w=T):
            return ps[:, b, 0:w]

        def kq_at(i, w):
            return (0, T) if i == 0 else (T + (i - 1) * w, w)

        def mix_w(l):
            return T if l == 0 else S

        def qcol(l, t, s, qt, h2):
            return (t * (mix_w(l) // P) + 2 * s + qt) * 2 + h2

        def attn_units(l):
            units = []
            g = 0
            for t in range(4):
                for s in range(1 if l else 2):
                    for h2 in range(2):
                        for qt in range(2):
                            units.append((g, s, t, h2, qt, range(4) if s == 0 else range(2, 4)))
                    g += 1
            return units

        S_BANK = [0, 1, 6, 7]
        def in_slot(l, i):
            return START[f"in{l}"] + (max(i, 3 * i - 2) if l == 0 else i)

        FREE_ORDER = {0: [4, 5, 6, 7, 0, 1, 2, 3], 3: [6, 7, 0, 1, 2, 3, 4, 5]}
        OUT_K = [4, 5, 6, 7, 0, 1, 2, 3]

        block = ctx.enter_context(nc.Block())

        @block.sync
        def _(sp):
            sp.dma_start(cvec[:], cvec_in).then_inc(cond_loaded, 16)
            sp.dma_start(ada_b[:], ada_b_in).then_inc(cond_loaded, 16)
            for r in range(RING):
                sp.dma_start(raw[:, r, :], stream[r]).then_inc(raw_loaded[r], 16)
            sp.dma_start(X[:], x_in).then_inc(x_loaded, 16)
            sp.dma_start(vec[:], vec_in).then_inc(vec_loaded, 16)
            sp.dma_start(ident[:], ident_in).then_inc(vec_loaded, 16)
            with sp.Fori(1, N_SLOTS // RING) as i:
                for r in range(RING):
                    sp.wait_ge(w_ready, i * RING + (r + 1 - RING))
                    sp.dma_start(raw[:, r, :], stream[bass.ds(i * RING + r, 1), :, :].rearrange("a p n -> (a p) n")
                                 ).then_inc(raw_loaded[r], 16)
            for m in range(KD):
                sp.wait_ge(x_new, LAST_EPOCH * KD + m + 1)
                sp.dma_start(out[:, m, :], X[:, m, 0:S]).then_inc(out_sem, 16)
            sp.wait_ge(out_sem, 16 * KD)

        @block.tensor
        def _(pe):
            c = Tally()
            pe.sem_inc(slots_done, RING)

            def weights(at, dyn=0):
                pe.wait_ge(w_ready, dyn + (at + 1))

            def mm3(dst, at, tile, rhs_hi, rhs_lo, start, stop):
                r = at % RING
                w1 = whi[:, r, tile * P:(tile + 1) * P]
                w2 = wlo[:, r, tile * P:(tile + 1) * P]
                pe.matmul(dst, w1, rhs_hi, start=start, stop=False)
                pe.matmul(dst, w1, rhs_lo, start=False, stop=False)
                return pe.matmul(dst, w2, rhs_hi, start=False, stop=stop)

            def norm(w, split=True, begun=False):
                if not begun:
                    norm_sums(w)
                c["rms"] += 1
                c["root"] += 1
                pe.wait_ge(rstd_ready, c["root"])
                spread(tok_rstd, w, 7).then_inc(rows_ready, 1)
                c["nl"] += KD if split else 0

            def norm_sums(w):
                c["norm"] += 1
                pe.wait_ge(all_added, c["norm"])
                for n in range(w // P):
                    last = pe.matmul(ps[:, 0, n:n + 1], sqsum[:, n * P:(n + 1) * P], ones[:, 0:1],
                                     start=True, stop=True)
                last.then_inc(sq_summed, 1)

            def spread(cols, w, b, at=0):
                for n in range(w // P):
                    last = pe.transpose(ps[:, b, at + n * P:at + (n + 1) * P],
                                        cols[:, n:n + 1].to_broadcast([P, P]), ident[:])
                return last

            def input_sums():
                c["cols"] += 1
                pe.wait_ge(sq_added, KD * c["cols"])
                for n in range(2):
                    last = pe.matmul(ps[:, 7, n:n + 1], sqsum[:, n * P:(n + 1) * P], ones[:, 0:1],
                                     start=True, stop=True)
                last.then_inc(col_sums, 1)

            def input_rows(root):
                c["rms"] += 1
                pe.wait_ge(recip_done, c["rms"])
                last = spread(tok_inv, S, 6)
                if root:
                    c["root"] += 1
                    pe.wait_ge(rstd_ready, c["root"])
                    last = spread(tok_rstd, S, 6, S)
                last.then_inc(inv_spread, 1)

            def out_tile(dst, at, dyn, w, src_h, src_l, first=False, before_last=None):
                weights(at, dyn)
                for k in range(KD):
                    if k == KD - 1 and before_last:
                        before_last()
                    if first:
                        pe.wait_ge(nl_ready, c["nl"] - KD + k + 1)
                    last = mm3(dst, at, k, src_h[:, k, 0:w], src_l[:, k, 0:w], k == 0, k == KD - 1)
                last.then_inc(slots_done, 1)

            def joint_tiles(dst0, at0, dst1, at1, dyn, w):
                weights(max(at0, at1), dyn)
                for k in range(KD):
                    pe.wait_ge(nl_ready, c["nl"] - KD + k + 1)
                    one = mm3(dst0, at0, k, nh[:, k, 0:w], nl[:, k, 0:w], k == 0, k == KD - 1)
                    if k == KD - 1:
                        one.then_inc(slots_done, 1)
                    two = mm3(dst1, at1, k, nh[:, k, 0:w], nl[:, k, 0:w], k == 0, k == KD - 1)
                two.then_inc(slots_done, 1)

            def up4(at, dyn, unit, udyn, w, mlp):
                for u in range(2):
                    pe.wait_ge(up_evac, udyn + (unit + u + 1))
                    if u == 0 and not mlp:
                        joint_tiles(bank(0, w), at, bank(1, w), at + 1, dyn, w)
                        continue
                    for half in range(2):
                        if mlp:
                            dst = ps[:, u, half * S:(half + 1) * S]
                        else:
                            dst = bank(2 * u + half, w)
                        src_h, src_l = (bh, bl) if mlp else (nh, nl)
                        out_tile(dst, at + 2 * u + half, dyn, w, src_h, src_l)

            def ada(at, dyn, kt):
                weights(at, dyn)
                for b in range(2):
                    for w in (whi, wlo):
                        last = pe.matmul(bank(4 + b), cst4[:, 4 * kt:4 * kt + P],
                                         w[:, at % RING, b * 512:(b + 1) * 512],
                                         start=(kt == 0 and w is whi), stop=(kt == KD - 1 and w is wlo))
                last.then_inc(slots_done, 1)

            def ada_cols_free(g, gdyn):
                pe.wait_ge(ada_row_ready, gdyn + (g + 1))
                if g:
                    pe.wait_ge(mod_ready, gdyn + g)

            def ada_cols():
                for m in range(KD):
                    last = pe.transpose(ps[:, 6, 4 * m:4 * m + 4], ada_row[:, m * P:(m + 1) * P],
                                        ident[0:4, 0:4])
                last.then_inc(ada_cols_done, 1)

            def ffn_up(name, w, ada_groups):
                at = START[name]
                if ada_groups:
                    with pe.Fori(0, ada_groups) as i:
                        if c["ada"]:
                            pe.wait_ge(ada_row_ready, i + c["ada"])
                        for n, (what, q) in enumerate(ADA_GROUP):
                            if what == "ada":
                                ada(at + n, i * 16, q)
                            elif what == "gate":
                                pe.wait_ge(up_evac, i * 4 + (c["unit"] + q + 1))
                                if q == 0:
                                    joint_tiles(bank(0, w), at, bank(1, w), at + 1, i * 16, w)
                                else:
                                    out_tile(bank(2 * (q % 2), w), at + n, i * 16, w, nh, nl)
                            elif q:
                                out_tile(bank(2 * (q % 2) + 1, w), at + n, i * 16, w, nh, nl,
                                         before_last=(lambda: ada_cols_free(c["ada"], i)) if q == 3 else None)
                        ada_cols()
                    at += 16 * ada_groups
                    c["unit"] += 4 * ada_groups
                    c["ada"] += ada_groups
                left = (START[name.replace("up", "down")] - at) // 4
                with pe.Fori(0, left) as i:
                    up4(at, i * 4, c["unit"], i * 2, w, False)
                c["unit"] += 2 * left

            def mlp_up(name):
                at = START[name]
                c["nl"] += KD
                pe.wait_ge(up_evac, c["unit"] + 1)
                out_tile(bank(0, S), at, 0, S, bh, bl, first=True)
                out_tile(ps[:, 0, S:T], at + 1, 0, S, bh, bl)
                input_sums()
                pe.wait_ge(up_evac, c["unit"] + 2)
                out_tile(bank(1, S), at + 2, 0, S, bh, bl)
                input_rows(False)
                out_tile(ps[:, 1, S:T], at + 3, 0, S, bh, bl)
                with pe.Fori(0, NM // 4 - 1) as i:
                    up4(at + 4, i * 4, c["unit"] + 2, i * 2, S, True)
                c["unit"] += NM // 2

            def first_two(at, w, src_h, src_l, ready):
                weights(at + 1)
                pe.wait_ge(*ready)
                pe.wait_ge(up_evac, c["unit"] + 1)
                for k in range(2):
                    for m in (2, 3, 4, 5, 6, 7, 0):
                        mm3(bank(m, w), at + k, m, src_h(k, 0), src_l(k, 0), k == 0, False)
                pe.wait_ge(up_evac, c["unit"] + 2)
                for k in range(2):
                    mm3(bank(1, w), at + k, 1, src_h(k, 0), src_l(k, 0), k == 0, False
                        ).then_inc(slots_done, 1)

            def down_slot(at, dyn, k, kdyn, w, src_h, src_l, ready, first, last):
                weights(at, dyn)
                if ready is not None:
                    pe.wait_ge(*ready)
                order = [4, 5, 6, 7, 0, 1, 2, 3] if first else range(KD)
                for n, m in enumerate(order):
                    if first and n == 4:
                        pe.wait_ge(up_evac, c["unit"] + 1)
                    if first and n == 6:
                        pe.wait_ge(up_evac, c["unit"] + 2)
                    ins = mm3(bank(m, w), at, m, src_h(k, kdyn), src_l(k, kdyn), first, last)
                    if last and m < KD - 1:
                        ins.then_inc(acc_done, 1)
                ins.then_inc(slots_done, 1)

            def last_two(at, k0, k1, w, src_h, src_l, ready):
                weights(at + 1)
                pe.wait_ge(*ready)
                for m in range(KD):
                    first = mm3(bank(m, w), at, m, src_h(k0, 0), src_l(k0, 0), False, False)
                    if m == KD - 1:
                        first.then_inc(slots_done, 1)
                    last = mm3(bank(m, w), at + 1, m, src_h(k1, 0), src_l(k1, 0), False, True)
                    last.then_inc(slots_done if m == KD - 1 else acc_done, 1)

            def down(name, n_k, w, src_h, src_l, per_unit):
                at = START[name]
                if not c["block2"]:
                    pe.wait_ge(mod_ready, c["ada"])
                base = c["hid"]

                def ready(k, kdyn):
                    return (hid_lo, kdyn + (base + k // per_unit + 3))

                if per_unit == 2:
                    first_two(at, w, src_h, src_l, ready(1, 0))
                for k in range(2 if per_unit == 2 else 0, 4):
                    down_slot(at + k, 0, k, 0, w, src_h, src_l, ready(k, 0), k == 0, False)
                tail = n_k % 4 or 4
                loops = (n_k - 4 - tail) // 4
                with pe.Fori(0, loops) as i:
                    for q in range(4):
                        down_slot(at + 4 + q, i * 4, 4 + q, i, w, src_h, src_l,
                                  ready(4 + q, i * (4 // per_unit)), False, False)
                for k in range(n_k - tail, n_k - 2):
                    down_slot(at + k, 0, k, 0, w, src_h, src_l, ready(k, 0), False, False)
                last_two(at + n_k - 2, n_k - 2, n_k - 1, w, src_h, src_l, ready(n_k - 1, 0))
                c["hid"] += n_k // per_unit

            def hid(buf, step, w, base=0):
                def at(k, kdyn):
                    if isinstance(kdyn, int):
                        return buf[:, base + k * step:base + k * step + w]
                    return buf[:, bass.ds(kdyn * (4 * step) + (base + k * step), w)]
                return at

            def short_down(name, w, src_h, src_l, order, readies, free=None):
                at = START[name]
                for n, k in enumerate(order[:-2]):
                    weights(at + n)
                    pe.wait_ge(*readies[n])
                    for m in (FREE_ORDER[free[2]] if n == 0 and free else range(KD)):
                        if n == 0 and free and m == free[2]:
                            pe.wait_ge(*free[:2])
                        ins = mm3(bank(m, w), at + n, m, src_h[:, k, 0:w], src_l[:, k, 0:w], n == 0, False)
                    ins.then_inc(slots_done, 1)
                n = len(order) - 2
                last_two(at + n, order[n], order[n + 1], w, lambda k, _: src_h[:, k, 0:w],
                         lambda k, _: src_l[:, k, 0:w], readies[n + 1])

            def attention(l):
                units = attn_units(l)
                w = mix_w(l)
                n = len(units)

                def scores(u):
                    g, s, t, h2, qt, kts = units[u]
                    if u >= 4:
                        pe.wait_ge(exp_ready, c["att"] + u - 3)
                    a, _ = kq_at(1 + t, w)
                    rows = slice(64 * h2, 64 * h2 + 64)
                    keys = slice(kts[0] * P, (kts[-1] + 1) * P)
                    nk = len(kts) * P
                    pe.matmul(ps[:, S_BANK[u % 4], 0:nk], kq[rows, a + s * S + qt * P:a + s * S + (qt + 1) * P],
                              kq[rows, keys], start=True, stop=True).then_inc(s_done, 1)

                def values(pair):
                    g, s, t, h2, _, kts = units[2 * pair]
                    pe.wait_ge(pts_ready, c["att"] + 2 * pair + 2)
                    if g >= 2:
                        pe.wait_ge(o_lo, c["og"] + g - 1)
                    for n_, kt in enumerate(kts):
                        last = pe.matmul(ps[64 * h2:64 * h2 + 64, 4 + g % 2, 0:S],
                                         vtok[:, kt, 64 * h2:64 * h2 + 64], probT[:, pair % 2, kt, :],
                                         start=(n_ == 0), stop=(n_ == len(kts) - 1))
                    last.then_inc(o_done, 1)

                pe.wait_ge(qk_ready, 5 * (l + 1))
                pe.wait_ge(vtok_ready, l + 1)
                pe.wait_ge(side_lo, 4 * (l + 1))
                for u in range(3):
                    scores(u)
                for u in range(n):
                    if u + 3 < n:
                        scores(u + 3)
                    if u >= 2:
                        pe.wait_ge(pts_ready, c["att"] + u - 1)
                    pe.wait_ge(prob_ready, c["att"] + u + 1)
                    kts = units[u][5]
                    for j in range(len(kts)):
                        last = pe.transpose(ps[:, 2 + u % 2, j * P:(j + 1) * P],
                                            prob[:, u % 4, j * P:(j + 1) * P], ident[:])
                    last.then_inc(pt_done, 1)
                    if u % 2 and u > 1:
                        values(u // 2 - 1)
                values(n // 2 - 1)
                c["att"] += n
                c["og"] += n // 4

            def mixer1(l):
                w = mix_w(l)

                def tile(i):
                    ww = T if i < 2 else w
                    if i >= 4:
                        pe.wait_ge(z_ready, 10 * l + i - 3)
                    out_tile(bank(i % 4, ww), in_slot(l, i), 0, ww, nh, nl)

                def rot(i, b):
                    a, _ = kq_at(i, w)
                    pe.matmul(bank(b, S), ccol("swap", 0, P), kq[:, a:a + S], start=True,
                              stop=True).then_inc(rot_done, 1)

                def channel_dft(u):
                    if u >= 2:
                        pe.wait_ge(ab_ready, c["f1"] + u - 1)
                    for ch in range(2):
                        last = pe.matmul(ps[:, u % 2, ch * 2 * P:(ch + 1) * 2 * P],
                                         zf[:, ch, u * P:(u + 1) * P], ccol("dft_c", 0, 2 * P),
                                         start=True, stop=True)
                    last.then_inc(f1_done, 1)

                joint_tiles(bank(0), in_slot(l, 0), bank(1), in_slot(l, 1), 0, T)
                for i in range(1, 9):
                    if i > 1:
                        tile(i)
                    if i == 2:
                        pe.wait_ge(mix_loaded, 48 * (l + 1))
                        pe.wait_ge(z_ready, 10 * l + 1)
                        pe.matmul(bank(7), ccol("blk", 0, P), kqs[:, 0:T], start=True,
                                  stop=True).then_inc(hssq_done, 1)
                    if i == 6:
                        pe.wait_ge(z_ready, 10 * l + 6)
                        pe.wait_ge(hms_read, 2 * l + 1)
                        pair = cst[:, CST["blk"]:CST["blk"] + P].rearrange("p (h n) -> p h n", n=HD)[:, :, 0]
                        for t in range(4):
                            a, _ = kq_at(1 + t, w)
                            for n in range(w // P):
                                o = 2 * (t * (w // P) + n)
                                last = pe.matmul(ps[:, 7, o:o + 2], kqs[:, a + n * P:a + (n + 1) * P], pair,
                                                 start=True, stop=True)
                        last.then_inc(hssq_done, 1)
                    if l == 0:
                        if i == 5:
                            ada_cols_free(c["ada"], 0)
                            ada_cols()
                            c["ada"] += 1
                            pe.wait_ge(ada_row_ready, c["ada"])
                        for n in range(2):
                            ada(in_slot(0, i) + 1 + n, 0, 2 * ((i - 1) % 4) + n)
                tile(9)
                if l == 0:
                    ada_cols_free(c["ada"], 0)
                    ada_cols()
                    c["ada"] += 1
                pe.wait_ge(zn_ready, l + 1)
                if l == 0:
                    pe.wait_ge(ada_row_ready, c["ada"])
                rot(0, 4)
                rot(1, 5)
                pe.wait_ge(z_ready, 10 * l + 10)
                pe.wait_ge(hms_read, 2 * l + 2)
                for kt in range(4):
                    last = pe.transpose(ps[:, 7, kt * P:(kt + 1) * P], zv[:, kt * P:(kt + 1) * P], ident[:])
                last.then_inc(vt_done, 1)
                channel_dft(0)
                channel_dft(1)
                for i in (2, 3):
                    pe.wait_ge(qk_ready, 5 * l + i - 1)
                    rot(i, 2 + i)
                for u in range(2, 2 * (w // S)):
                    channel_dft(u)
                if l == 0:
                    pe.wait_ge(mod_ready, c["ada"])
                rot(4, 6)
                pe.wait_ge(qk_ready, 5 * l + 4)
                for s in range(w // S):
                    pe.wait_ge(ab_ready, c["f1"] + 2 * s + 2)
                    for ch in range(2):
                        for tt in range(2):
                            for cs in range(2):
                                o = (tt * 2 + cs) * S
                                last = pe.matmul(bank(2 + 2 * s + ch, S),
                                                 ab[:, 2 * s + tt, ch, cs * P:(cs + 1) * P],
                                                 ccol("dft_s", o, o + S), start=(tt == 0 and cs == 0),
                                                 stop=(tt == 1 and cs == 1))
                        last.then_inc(f2_done, 1)
                c["f1"] += 2 * (w // S)
                c["f2"] += 2 * (w // S)
                pe.wait_ge(yt_ready, c["f2"])
                pe.wait_ge(qk_ready, 5 * (l + 1))
                pe.wait_ge(vtok_ready, l + 1)
                for m in range(2):
                    for k in range(2):
                        last = pe.matmul(bank(6 + m, w), fftw[:, k, m * P:(m + 1) * P], yt[:, k, 0:w],
                                         start=(k == 0), stop=(k == 1))
                    last.then_inc(side_done, 1)
                pe.wait_ge(ab_ready, c["f1"])
                pe.wait_ge(pool_ready, l + 1)
                for m in range(2):
                    pe.matmul(bank(m, w), poolw[:, m, :], pc[:, m, 0:w // S, :], start=True,
                              stop=True).then_inc(side_done, 1)
                attention(l)
                readies = ([(side_lo, 4 * (l + 1))] * 4
                           + [(o_lo, c["og"] - (w // S) * (3 - t)) for t in range(4)])
                pe.wait_ge(o_lo, c["og"])
                short_down(f"out{l}", w, nh, nl, OUT_K, readies)

            pe.wait_ge(consts_ready, 1)
            pe.wait_ge(cond_loaded, 32)
            pe.wait_ge(c_ready, 1)
            for g in range(2):
                if g:
                    pe.wait_ge(ada_row_ready, 1)
                for kt in range(KD):
                    if g and kt == KD - 1:
                        norm_sums(T)
                    ada(8 * g + kt, 0, kt)
                if g:
                    norm(T, begun=True)
                if g == 0:
                    pe.wait_ge(vec_loaded, 32)
                ada_cols_free(g, 0)
                ada_cols()
                c["ada"] += 1
            for l in range(DEPTH):
                if l:
                    norm(T)
                ffn_up(f"ffn1_up{l}", T, 5 if l == 0 else 4)
                down(f"ffn1_down{l}", NF, T, hid(hh, T, T), hid(hl, T, T), 1)
                norm(T)
                mixer1(l)
                w = mix_w(l)
                norm(w)
                ffn_up(f"ffn2_up{l}", w, 5 if l == 0 else 0)
                if w == T:
                    down(f"ffn2_down{l}", NF, w, hid(hh, T, w), hid(hl, T, w), 1)
                else:
                    down(f"ffn2_down{l}", NF, S, hid(hh, S, S), hid(hh, S, S, NF * S), 1)
            c["block2"] = 1
            norm(S, split=False)

            def rglru(i, j):
                at = START[f"b_in{i}"]
                c["nl"] += KD

                def tile(n):
                    if n >= 4:
                        pe.wait_ge(b_evac, c["bev"] + n - 3)
                    out_tile(bank(n % 4, S), at + n, 0, S, bh, bl, first=(n == 0))

                def gates(m):
                    if m == 0:
                        pe.wait_ge(gates_loaded, 16 * (j + 1))
                    pe.wait_ge(cv_ready, c["cv"] + min(NR, m + 2))
                    if m >= 2:
                        pe.wait_ge(gate_ready, c["cv"] + m - 1)
                    for g in range(2):
                        for n, k in enumerate(GATE_K[m]):
                            last = pe.matmul(ps[:, 4 + m % 2, g * S:(g + 1) * S],
                                             gates_w[:, g, GATE_BLOCKS.index((k, m)), :], cv[:, k, :], start=(n == 0), stop=(n == len(GATE_K[m]) - 1))
                    last.then_inc(gate_mm, 1)

                for n in range(HEAD_G):
                    tile(n)
                    if n == 1:
                        input_sums()
                    if n == 2:
                        input_rows(True)
                for m in range(NR):
                    tile(HEAD_G + m)
                    if m >= 2:
                        gates(m - 2)
                for n in range(HEAD_G + NR, 2 * NR):
                    tile(n)
                    if n < HEAD_G + NR + 2:
                        gates(n - HEAD_G - 2)
                c["cv"] += NR
                c["bev"] += 2 * NR
                pe.wait_ge(gate_ready, c["cv"])
                short_down(f"b_out{i}", S, oh, ol, range(NR), [(b_lo, c["blo"] + k + 1) for k in range(NR)],
                           free=(b_evac, c["bev"], 0))
                c["blo"] += NR

            def sgu(i):
                at = START[f"b_in{i}"]
                c["nl"] += KD

                def tile(n):
                    if n >= 4:
                        pe.wait_ge(b_evac, c["bev"] + n - 3)
                    out_tile(bank(n % 4, S), at + n, 0, S, bh, bl, first=(n == 0))

                def turn(m):
                    pe.wait_ge(vg_scaled, m + 1)
                    if m >= 2:
                        pe.wait_ge(vtt_ready, m - 1)
                    for n in range(2):
                        last = pe.transpose(ps[:, 4 + m % 2, n * P:(n + 1) * P], vg[:, m, n * P:(n + 1) * P],
                                            ident[:])
                    last.then_inc(vtt_done, 1)

                def mix(m):
                    pe.wait_ge(vtt_ready, m + 1)
                    if m >= 2:
                        pe.wait_ge(b_f32, c["blo"] + m - 1)
                    for n in range(2):
                        dst = ps[:, 6 + m % 2, n * P:(n + 1) * P]
                        pe.matmul(dst, vt[:, m, n * P:(n + 1) * P], ws[:, m, :], start=True, stop=False)
                        last = pe.matmul(dst, ones[0:1, :], sbias[:, m * P:(m + 1) * P], start=False, stop=True)
                    last.then_inc(mixd_done, 1)

                for n in range(KD):
                    tile(n)
                    if n == 1:
                        input_sums()
                    if n == 2:
                        input_rows(True)
                pe.wait_ge(row_copied, c["cols"])
                pe.wait_ge(ws_ready, 1)
                pe.wait_ge(small_loaded, 32)
                for m in range(KD):
                    tile(KD + m)
                    if m == 0:
                        pe.wait_ge(v_added, KD)
                        for n in range(2):
                            last = pe.matmul(ps[:, 4, n:n + 1], sqsum[:, n * P:(n + 1) * P], ones[:, 0:1],
                                             start=True, stop=True)
                        last.then_inc(col_sums, 1)
                        c["rms"] += 1
                        c["root"] += 1
                    if m == 1:
                        pe.wait_ge(recip_done, c["rms"])
                    for k in SGU_MIX[m]:
                        mix(k)
                    for k in SGU_TURN[m]:
                        turn(k)
                c["bev"] += 2 * KD
                pe.wait_ge(b_f32, c["blo"] + KD)
                short_down(f"b_out{i}", S, oh, ol, range(KD), [(b_lo, c["blo"] + k + 1) for k in range(KD)],
                           free=(b_evac, c["bev"], 0))
                c["blo"] += KD

            def conv(i):
                at = START[f"b_in{i}"]
                c["nl"] += KD
                for m in range(KD):
                    if m >= 2:
                        pe.wait_ge(b_f32, c["blo"] + m - 1)
                    for q in range(3):
                        b = 3 * (m % 2) + q
                        out_tile(bank(b, S), at + 3 * m + q, 0, S, bh, bl, first=(m == 0 and q == 0))
                        if m == 0 and q == 1:
                            input_sums()
                        if m == 0 and q == 2:
                            input_rows(True)
                short_down(f"b_out{i}", S, oh, ol, range(KD), [(b_lo, c["blo"] + k + 1) for k in range(KD)],
                           free=(b_f32, c["blo"] + KD, 3))
                c["blo"] += KD

            for i, kind in enumerate(MIXERS):
                if kind == "rglru":
                    rglru(i, i // 3)
                elif kind == "sgu":
                    sgu(i)
                else:
                    conv(i)
                mlp_up(f"mlp_up{i}")
                down(f"mlp_down{i}", NM, S, hid(mh, S, S), hid(ml, S, S), 2)
            norm(S, split=False)

        @block.scalar
        def _(act):
            c = Tally()

            def split(at, dyn=0):
                if at >= N_SLOTS:
                    return
                r = at % RING
                act.wait_ge(raw_loaded[r], dyn * 4 + 16 * (at // RING + 1))
                act.wait_ge(slots_done, dyn + (at + 1))
                act.activation(whi[:, r, :], raw[:, r, :], ACT.Copy).then_inc(w_hi_ready, 1)

            def split_to(at):
                while c["split"] <= at:
                    split(c["split"])
                    c["split"] += 1

            def late_split():
                if c["late"]:
                    split_to(c["split"])
                    c["late"] = 0

            def done(at, dyn=0):
                act.wait_ge(slots_done, dyn + (RING + at + 1))

            def square(m, w):
                act.wait_ge(x_new, c["x"] + m + 1)
                if m >= 4:
                    act.wait_ge(part_added, c["part"] + m - 4 + (m == 4))
                act.activation(norm_buf(m)[:, 0:w], X[:, m, 0:w], ACT.Square).then_inc(sq_ready, 1)

            def squared():
                c["x"] += KD
                c["part"] += KD - 3

            def norm(w, ord_shift=None, dst=None, split_out=True, begun=False):
                if not begun:
                    act.preload_act_table(ACT.Sqrt)
                    for m in range(KD):
                        square(m, w)
                    squared()
                    late_split()
                    root(w)
                if not split_out:
                    return
                act.wait_ge(mod_ready, ord_shift + 1)
                for m in range(KD):
                    act.wait_ge(y_ready, c["y"] + m + 1)
                    for s in range(w // S):
                        last = act.activation(dst[:, m, s * S:(s + 1) * S], tmpb[:, m % 2, s * S:(s + 1) * S],
                                              ACT.Identity, bias=mod[:, ord_shift, m, s:s + 1])
                    last.then_inc(nh_ready, 1)
                c["y"] += KD

            def root(w):
                c["rms"] += 1
                c["root"] += 1
                act.wait_ge(recip_done, c["rms"])
                act.activation(tok_rstd[:, 0:w // P], tok_inv[:, 0:w // P], ACT.Sqrt).then_inc(rstd_ready, 1)

            def upper_gain(gain):
                for m in range(KD):
                    act.wait_ge(x_new, c["x"] + m + 1)
                    act.activation(bh[:, m, :], X[:, m, 0:S], ACT.Copy, scale=vcol(*gain(m))).then_inc(nh_ready, 1)
                    if c["sb"] + m >= 4:
                        act.wait_ge(sq_added, c["sb"] + m - 3)
                    act.activation(square_buf(m), X[:, m, 0:S], ACT.Square).then_inc(sq_ready, 1)
                c["x"] += KD
                c["sb"] += KD
                late_split()

            def copy_rows(root):
                c["rows"] += 1
                act.wait_ge(inv_spread, c["rows"])
                act.activation(inv_row[:, 0:S], bank(6, S), ACT.Copy)
                if root:
                    last = act.activation(rstd_row[:], ps[:, 6, S:T], ACT.Copy)
                else:
                    last = act.activation(inv_row[:, S:T], bank(6, S), ACT.Copy)
                last.then_inc(row_copied, 1)

            def unit(at, dyn, u, udyn, w, mlp, local, ldyn, between=None):
                done(at + 1 if mlp else at, dyn)
                act.wait_ge(up_evac, udyn + (u + 1))
                if mlp:
                    act.activation(tmpa[:, u % 2, :], ps[:, u % 2, :], ACT.Relu).then_inc(up_act, 1)
                    w, dst = T, mh
                else:
                    act.activation(tmpa[:, u % 2, 0:w], bank(2 * (u % 2), w), ACT.Silu).then_inc(up_act, 1)
                    dst = hh
                if between:
                    between()
                act.wait_ge(up_evac, udyn + (u + 3))
                act.activation(dst[:, bass.ds(ldyn * w + local * w, w)], tmpb[:, u % 2, 0:w],
                               ACT.Copy).then_inc(hid_hi, 1)

            def up4(at, dyn, u, udyn, w, mlp, local, ldyn):
                for q in range(2):
                    split(at + 3 + 2 * q, dyn)
                    unit(at + 2 * q, dyn, u + q, udyn, w, mlp, local + q, ldyn,
                         between=lambda: split(at + 4 + 2 * q, dyn))

            def ada_rows(g, gdyn):
                if g:
                    act.wait_ge(ada_cols_done, gdyn + g)
                act.activation(ada_row[:].rearrange("p (a b) -> p a b", a=2), ps[0:4, 4:6, :],
                               ACT.Copy).then_inc(ada_row_ready, 1)

            def ffn_up(name, w, ada_groups):
                at = START[name]
                act.preload_act_table(ACT.Silu)
                local = 0
                if ada_groups:
                    with act.Fori(0, ada_groups) as i:
                        for u in range(4):
                            for q in range(4):
                                split(at + 4 * u + q + 3, i * 16)
                            if u == 3:
                                done(at + 14, i * 16)
                                ada_rows(c["ada"], i)
                            unit(at + ADA_GROUP.index(("gate", u)), i * 16, c["unit"] + u, i * 4, w, False, u, i * 4)
                    at += 16 * ada_groups
                    c["unit"] += 4 * ada_groups
                    c["ada"] += ada_groups
                    local = 4 * ada_groups
                left = (START[name.replace("up", "down")] - at) // 4
                with act.Fori(0, left) as i:
                    up4(at, i * 4, c["unit"], i * 2, w, False, local, i * 2)
                c["unit"] += 2 * left
                c["split"] = at + 4 * left + 3

            def mlp_up(name):
                at = START[name]
                split(at + 3)
                split(at + 4)
                copy_rows(False)
                unit(at, 0, c["unit"], 0, S, True, 0, 0)
                split(at + 5)
                split(at + 6)
                unit(at + 2, 0, c["unit"] + 1, 0, S, True, 1, 0)
                with act.Fori(0, NM // 4 - 1) as i:
                    up4(at + 4, i * 4, c["unit"] + 2, i * 2, S, True, 2, i * 2)
                c["unit"] += NM // 2
                c["split"] = START[name] + NM + 3

            def down(name, n_k):
                at = START[name]
                loops = n_k // 4 - 1
                with act.Fori(0, loops) as i:
                    for q in range(4):
                        split(at + 3 + q, i * 4)
                c["split"] = at + 3 + 4 * loops
                split_to(at + n_k + 1)
                c["late"] = 1

            def short_down(name, n_k):
                split_to(START[name] + n_k + 1)
                c["late"] = 1

            def attention(l):
                units = attn_units(l)
                n = len(units)

                def turned(u):
                    pair, (g, s, t, h2, qt, kts) = u // 2, units[u]
                    act.wait_ge(pt_done, c["att"] + u + 1)
                    if pair >= 2:
                        act.wait_ge(o_done, c["op"] + pair - 1)
                    act.activation(probT[:, pair % 2, kts[0]:kts[-1] + 1, qt * P:(qt + 1) * P],
                                   ps[:, 2 + u % 2, 0:len(kts) * P].rearrange("p (k q) -> p k q", q=P),
                                   ACT.Copy).then_inc(pts_ready, 1)

                def o_upper(g):
                    _, s, t, *_ = units[4 * g]
                    act.wait_ge(o_done, c["op"] + 2 * g + 2)
                    act.activation(nh[:, t, s * S:(s + 1) * S], bank(4 + g % 2, S), ACT.Copy).then_inc(o_hi, 1)

                for u, (g, s, t, h2, qt, kts) in enumerate(units):
                    nk = len(kts) * P
                    act.wait_ge(nmax_ready, c["att"] + u + 1)
                    if u >= 4:
                        act.wait_ge(pt_done, c["att"] + u - 3)
                    q = qcol(l, t, s, qt, h2)
                    act.activation(prob[:, u % 4, 0:nk], ps[:, S_BANK[u % 4], 0:nk], ACT.Exp, bias=snm[:, u:u + 1],
                                   scale=qscale[:, 0, q:q + 1], accum_out=ssm[:, u:u + 1]).then_inc(exp_ready, 1)
                    if u > 1:
                        turned(u - 2)
                    if u >= 6 and u % 4 == 2:
                        o_upper(u // 4 - 1)
                turned(n - 2)
                turned(n - 1)
                o_upper(n // 4 - 1)
                c["att"] += n
                c["op"] += n // 2

            def mixer1(l):
                w = mix_w(l)
                for i in range(IN_TILES):
                    split_to(in_slot(l, i) + 3)
                    if i == 5:
                        act.wait_ge(hrecip, 2 * l + 1)
                        act.activation(kqs[:, 0:T], kqs[:, 0:T], ACT.Sqrt).then_inc(hrstd, 1)
                    if i == 8:
                        n = 8 * (w // P)
                        act.wait_ge(hrecip, 2 * l + 2)
                        act.activation(qscale[:, 0, 0:n], qinv[:, 1, 0:n], ACT.Sqrt,
                                       scale=ATTN_SCALE ** 2).then_inc(hrstd, 1)
                    if l == 0 and i in (5, 9):
                        done(in_slot(l, i) - 1)
                        ada_rows(c["ada"], 0)
                        c["ada"] += 1
                    done(in_slot(l, i))
                    ww = T if i < 2 else w
                    src = bank(i % 4, ww)
                    if i == 0 or 2 <= i < 6:
                        a, _ = kq_at(i - 1 if i else 0, w)
                        act.activation(kq[:, a:a + ww], src, ACT.Copy,
                                       scale=vcol("q_gain" if i else "k_gain", l))
                        act.activation(kqs[:, a:a + ww], src, ACT.Square).then_inc(z_ready, 1)
                    elif i == 1:
                        act.activation(zv[:], src, ACT.Copy).then_inc(z_ready, 1)
                    elif i < 8:
                        act.wait_ge(pads_ready, l + 1)
                        act.activation(up[:, i - 6, 0:w // S, 8:8 + S], src.rearrange("p (s t) -> p s t", t=S),
                                       ACT.Copy).then_inc(z_ready, 1)
                    else:
                        act.activation(zf[:, i - 8, 0:w], src, ACT.Copy).then_inc(z_ready, 1)
                act.preload_act_table(ACT.Exp)
                act.wait_ge(hrstd, 2 * l + 2)
                act.wait_ge(vt_done, l + 1)
                act.activation(vtok[:].rearrange("p a b -> p (a b)"), bank(7), ACT.Copy).then_inc(vtok_ready, 1)
                for m in range(2):
                    act.wait_ge(side_done, 4 * l + m + 1)
                    act.activation(nh[:, 6 + m, 0:w], bank(6 + m, w), ACT.Copy).then_inc(side_hi, 1)
                for m in range(2):
                    act.wait_ge(side_done, 4 * l + m + 3)
                    act.activation(nh[:, 4 + m, 0:w], bank(m, w), ACT.Identity,
                                   scale=vcol("pool_scale", 2 * l + m)).then_inc(side_hi, 1)
                attention(l)
                short_down(f"out{l}", KD)

            lam = vec[:, VEC["lam"]:VEC["lam"] + 2 * NR]

            def softplus():
                act.activation(sp_t[:, 0, :], lam, ACT.Abs).then_inc(act_chain, 1)
                act.wait_ge(act_chain, 1)
                act.activation(sp_t[:, 1, :], sp_t[:, 0, :], ACT.Exp, scale=-1.0).then_inc(sp_step, 1)

            act.wait_ge(cond_loaded, 32)
            act.activation(csil[:].rearrange("p k c -> p (k c)"), cvec[:].rearrange("p k c -> p (k c)"),
                           ACT.Silu).then_inc(csil_ready, 1)
            act.wait_ge(csil_ready, 1)
            act.wait_ge(consts_ready, 1)
            act.activation(cst4[:, 0:32].rearrange("p (k c) -> p k c", c=4)[:, :, 0:2], csil[:],
                           ACT.Copy).then_inc(c_hi_ready, 1)
            for g in range(2):
                split_to(10)
                if g:
                    for n in range(4):
                        split_to(11 + n)
                        square(2 * n, T)
                        square(2 * n + 1, T)
                    squared()
                    split_to(15)
                    act.preload_act_table(ACT.Sqrt)
                    split_to(17)
                    root(T)
                    split_to(18)
                done(8 * g + 7)
                ada_rows(g, 0)
                c["ada"] += 1
            act.wait_ge(vec_loaded, 32)
            for l in range(DEPTH):
                norm(T, MOD(l, 0), nh, begun=(l == 0))
                ffn_up(f"ffn1_up{l}", T, 5 if l == 0 else 4)
                if l == 0:
                    softplus()
                down(f"ffn1_down{l}", NF)
                norm(T, MOD(l, 3), nh)
                mixer1(l)
                w = mix_w(l)
                norm(w, MOD(l, 6), nh)
                ffn_up(f"ffn2_up{l}", w, 5 if l == 0 else 0)
                down(f"ffn2_down{l}", NF)
            norm(S, split_out=False)
            def b_upper(dst, m):
                act.wait_ge(b_f32, c["b"] + m + 1)
                act.activation(dst[:, m, :], tmpb[:, m % 2, 0:S], ACT.Copy).then_inc(b_hi, 1)

            def rglru(i, j):
                at = START[f"b_in{i}"]
                split_to(at + 3)
                act.preload_act_table(ACT.Sqrt)
                split_to(at + 4)
                root(S)
                act.preload_act_table(ACT.Gelu_apprx_tanh)

                def gate_part(n, lag=0):
                    g = n if n < HEAD_G else n - NR
                    split_to(at + n + 3 + lag)
                    act.wait_ge(b_evac, c["bev"] + n + 1)
                    act.activation(gelu_g[:, g, :], gelu_g[:, g, :], ACT.Gelu_apprx_tanh).then_inc(gelu_ready, 1)

                def sigmoids(m):
                    act.wait_ge(gate_mm, c["cv"] + m + 1)
                    if m >= 2:
                        act.wait_ge(ix_ready, 3 * c["cv"] + 2 * (m - 2) + 1)
                        act.wait_ge(th_ready, c["cv"] + m - 1)
                    act.activation(sg[:, m % 2, 0:S], ps[:, 4 + m % 2, 0:S], ACT.Sigmoid,
                                   bias=vcol("ba", j * NR + m))
                    act.activation(sg[:, m % 2, S:T], ps[:, 4 + m % 2, S:T], ACT.Sigmoid,
                                   bias=vcol("bx", j * NR + m)).then_inc(gate_ready, 1)
                    act.wait_ge(gate_ready, c["cv"] + m + 1)
                    act.activation(th[:, m, :], sg[:, m % 2, 0:S], ACT.Tanh,
                                   scale=n4sp[:, j * NR + m:j * NR + m + 1]).then_inc(th_ready, 1)

                split_to(at + 5)
                copy_rows(True)
                for n in range(HEAD_G):
                    gate_part(n, 1)
                act.preload_act_table(ACT.Sigmoid)
                act.wait_ge(sp_step, 2)
                for m in range(NR):
                    split_to(at + HEAD_G + m + 3)
                    act.wait_ge(b_evac, c["bev"] + HEAD_G + m + 1)
                    act.activation(cv[:, m, :], xpad[:, m % 2, 3:3 + S], ACT.Identity,
                                   scale=vcol("conv_w", (j * 4 + 3) * NR + m),
                                   bias=vcol("conv_b", j * NR + m)).then_inc(cv_begun, 1)
                    if m >= 2:
                        sigmoids(m - 2)
                tail = HEAD_G + NR
                split_to(at + tail + 3)
                sigmoids(NR - 2)
                split_to(at + tail + 4)
                sigmoids(NR - 1)
                split_to(at + tail + 5)
                c["cv"] += NR
                act.preload_act_table(ACT.Sqrt)
                for h in range(2):
                    act.wait_ge(av_ready, c["cv"] - NR + 5 * h + 5)
                    act.activation(th[:, 5 * h:5 * h + 5, :], th[:, 5 * h:5 * h + 5, :], ACT.Sqrt,
                                   scale=-4.0).then_inc(root_ready, 1)
                act.preload_act_table(ACT.Gelu_apprx_tanh)
                for n in range(tail, 2 * NR):
                    gate_part(n, 1)
                    for m in RNN_TAIL[n - tail]:
                        b_upper(oh, m)
                c["bev"] += 2 * NR
                for m in range(RNN_TAIL[-1][-1] + 1, NR):
                    split_to(START[f"b_out{i}"] + m - 1)
                    b_upper(oh, m)
                c["b"] += NR
                short_down(f"b_out{i}", NR)

            def sgu(i):
                at = START[f"b_in{i}"]
                split_to(at + 3)
                act.preload_act_table(ACT.Sqrt)
                split_to(at + 4)
                root(S)
                act.preload_act_table(ACT.Gelu_apprx_tanh)

                def turned(m):
                    act.wait_ge(vtt_done, m + 1)
                    for n in range(2):
                        last = act.activation(vt[:, m, n * P:(n + 1) * P], ps[:, 4 + m % 2, n * P:(n + 1) * P],
                                              ACT.Copy, scale=tok_rstd[:, n:n + 1])
                    last.then_inc(vtt_ready, 1)

                split_to(at + 5)
                copy_rows(True)
                for m in range(KD):
                    split_to(at + m + 4)
                    act.wait_ge(b_evac, c["bev"] + m + 1)
                    act.activation(vg[:, m, :], zrow[:, m % 2, :], ACT.Gelu_apprx_tanh).then_inc(gelu_ready, 1)
                    if m >= 2:
                        act.wait_ge(v_added, m - 1)
                    act.wait_ge(gelu_ready, c["gelu"] + m + 1)
                    act.activation(vsq[:, m % 2, :], vg[:, m, :], ACT.Square).then_inc(vsq_ready, 1)
                for m in range(KD):
                    split_to(at + KD + m + 4)
                    act.wait_ge(b_evac, c["bev"] + KD + m + 1)
                    act.activation(ug[:, m, :], zrow[:, m % 2, :], ACT.Gelu_apprx_tanh).then_inc(gelu_ready, 1)
                    if m == 0:
                        act.preload_act_table(ACT.Sqrt)
                        root(S)
                        act.preload_act_table(ACT.Gelu_apprx_tanh)
                        act.wait_ge(rstd_ready, c["root"])
                    for k in SGU_TURN[m]:
                        turned(k)
                    for k in SGU_GATED[m]:
                        b_upper(oh, k)
                c["b"] += KD
                short_down(f"b_out{i}", KD)

            def conv(i):
                at = START[f"b_in{i}"]
                split_to(at + 3)
                act.preload_act_table(ACT.Sqrt)
                split_to(at + 4)
                root(S)
                split_to(at + 5)
                copy_rows(True)
                for m in range(KD):
                    split_to(at + 3 * m + 6)
                    b_upper(oh, m)
                c["b"] += KD
                short_down(f"b_out{i}", KD)

            for i, kind in enumerate(MIXERS):
                upper_gain(lambda m, i=i: ("norm_mix", i * KD + m))
                if kind == "rglru":
                    rglru(i, i // 3)
                    c["gelu"] += NR
                elif kind == "sgu":
                    sgu(i)
                    c["gelu"] += 2 * KD
                    c["bev"] += 2 * KD
                else:
                    conv(i)
                upper_gain(lambda m, i=i: ("norm_mlp", i * KD + m))
                c["rms"] += 1
                mlp_up(f"mlp_up{i}")
                down(f"mlp_down{i}", NM)
            act.wait_ge(sq_added, c["sb"])
            norm(S, split_out=False)

        @block.vector
        def _(dve):
            c = Tally()

            def link(ins):
                c["chain"] += 1
                ins.then_inc(dve_chain, 1)
                dve.wait_ge(dve_chain, c["chain"])

            def split(at, dyn=0):
                if at >= N_SLOTS:
                    return
                r = at % RING
                dve.wait_ge(w_hi_ready, dyn + (at + 1))
                dve.tensor_tensor(wlo[:, r, :], raw[:, r, :], whi[:, r, :].bitcast(F32),
                                  ALU.subtract).then_inc(w_ready, 1)

            def split_to(at):
                while c["split"] <= at:
                    split(c["split"])
                    c["split"] += 1

            def late_split():
                if c["late"]:
                    split_to(c["split"])
                    c["late"] = 0

            def done(at, dyn=0):
                dve.wait_ge(slots_done, dyn + (RING + at + 1))

            def mean_square(b, w):
                cols = w // P
                link(dve.tensor_scalar(tok_inv[:, 4:4 + cols], ps[:, b, 0:cols], 1.0 / D, EPS, ALU.mult, ALU.add))
                dve.reciprocal(tok_inv[:, 0:cols], tok_inv[:, 4:4 + cols]).then_inc(recip_done, 1)

            def add_last(w):
                c["sq"] += 1
                c["part"] += KD - 3
                dve.wait_ge(part_added, c["part"])
                squares = c["sq"] * KD + 2 * len(MIXERS) * KD * (c["sq"] == NORMS)
                dve.wait_ge(sq_ready, squares - 1)
                link(dve.tensor_tensor(sqsum[:, 0:w], sqsum[:, 0:w], norm_buf(KD - 2)[:, 0:w], ALU.add))
                dve.wait_ge(sq_ready, squares)
                dve.tensor_tensor(sqsum[:, 0:w], sqsum[:, 0:w], norm_buf(KD - 1)[:, 0:w],
                                  ALU.add).then_inc(all_added, 1)

            def inv_of_sums(w):
                c["root"] += 1
                dve.wait_ge(sq_summed, c["sq"])
                mean_square(0, w)

            def rstd_rows(w):
                add_last(w)
                late_split()
                inv_of_sums(w)

            def input_inv():
                c["cols"] += 1
                dve.wait_ge(col_sums, c["cols"])
                mean_square(7, S)

            def halves(w):
                return [slice(s * S, (s + 1) * S) for s in range(w // S)]

            def norm_mod(w, l, ord_shift, scale_at, begun=False):
                if not begun:
                    rstd_rows(w)
                dve.wait_ge(rows_ready, c["root"])

                def lower(m):
                    dve.wait_ge(nh_ready, c["y"] + m + 1)
                    for s, part in enumerate(halves(w)):
                        last = dve.scalar_tensor_tensor(
                            out=nl[:, m, part], in0=tmpb[:, m % 2, part], scalar=mod[:, ord_shift, m, s:s + 1],
                            in1=nh[:, m, part].bitcast(F32), op0=ALU.add, op1=ALU.subtract)
                    last.then_inc(nl_ready, 1)

                for m in range(KD):
                    if m >= 2:
                        dve.wait_ge(nl_ready, c["y"] + m - 1)
                    for s, part in enumerate(halves(w)):
                        last = dve.scalar_tensor_tensor(
                            out=tmpb[:, m % 2, part], in0=X[:, m, part], scalar=fix[:, scale_at, m, s:s + 1],
                            in1=ps[:, 7, part], op0=ALU.mult, op1=ALU.mult)
                    last.then_inc(y_ready, 1)
                    if m:
                        lower(m - 1)
                lower(KD - 1)
                c["y"] += KD

            def lower_gain(m, gain):
                dve.wait_ge(nh_ready, c["y"] + m + 1)
                dve.scalar_tensor_tensor(out=bl[:, m, :], in0=X[:, m, 0:S], scalar=vcol(*gain(m)),
                                         in1=bh[:, m, :].bitcast(F32), op0=ALU.mult,
                                         op1=ALU.subtract).then_inc(nl_ready, 1)

            def norm_last(name, gain=None):
                rstd_rows(S)
                dve.wait_ge(rows_ready, c["root"])
                for m in range(KD):
                    dve.scalar_tensor_tensor(out=X[:, m, 0:S], in0=X[:, m, 0:S], scalar=vcol(name, m),
                                             in1=bank(7, S), op0=ALU.mult, op1=ALU.mult).then_inc(x_new, 1)
                    if gain and m >= 2:
                        lower_gain(m - 2, gain)
                if gain:
                    lower_gain(KD - 2, gain)
                    lower_gain(KD - 1, gain)
                    c["y"] += KD

            def fix_one(l, k, g):
                n = MOD(l, g)
                dve.wait_ge(mod_ready, n + 1)
                op, val = (ALU.add, 1.0) if k < 3 else (ALU.mult, 0.5)
                link(dve.tensor_scalar(fix[:, 5 * l + k, :, :], mod[:, n, :, :], val, None, op))

            def residual(name, w, gate, gain=None):
                end = START[name] + dict(PLAN)[name] - 1
                for m in range(KD):
                    if m < KD - 1:
                        dve.wait_ge(acc_done, c["acc"] + m + 1)
                    else:
                        done(end)
                    if gate is None:
                        last = dve.tensor_tensor(X[:, m, 0:S], bank(m, S), X[:, m, 0:S], ALU.add)
                    else:
                        for s, part in enumerate(halves(w)):
                            last = dve.scalar_tensor_tensor(
                                out=X[:, m, part], in0=ps[:, m, part], scalar=gate[:, m, s:s + 1],
                                in1=X[:, m, part], op0=ALU.mult, op1=ALU.add)
                    last.then_inc(x_new, 1)
                    if gain and m >= 2:
                        lower_gain(m - 2, gain)
                if gain:
                    lower_gain(KD - 2, gain)
                    lower_gain(KD - 1, gain)
                    c["y"] += KD
                    late_split()
                c["acc"] += KD - 1

            def unit(u, udyn, w, mlp, local, ldyn, between=None):
                dve.wait_ge(up_act, udyn + (u + 1))
                if mlp:
                    w = T
                    src = tmpb[:, u % 2, :]
                else:
                    src = bank(2 * (u % 2) + 1, w)
                dve.wait_ge(hid_lo, udyn + (u + 1))
                if mlp:
                    dve.scalar_tensor_tensor(out=src, in0=ps[:, u % 2, :], scalar=0.0, in1=inv_row[:],
                                             op0=ALU.max, op1=ALU.mult).then_inc(relu_scaled, 1)
                    dve.wait_ge(relu_scaled, udyn + (u - c["ffn_units"] + 1))
                dve.tensor_tensor(tmpb[:, u % 2, 0:w], tmpa[:, u % 2, 0:w], src, ALU.mult).then_inc(up_evac, 1)
                if between:
                    between()
                if not mlp:
                    lower(u, udyn, w, False, local, ldyn)

            def lower(u, udyn, w, mlp, local, ldyn):
                w, h, l_ = (T, mh, ml) if mlp else (w, hh, hl if w == T else hh)
                dve.wait_ge(hid_hi, udyn + (u + 1))
                cols = bass.ds(ldyn * w + local * w, w)
                low = cols if w == T else bass.ds(ldyn * w + (NF * S + local * w), w)
                dve.tensor_tensor(l_[:, low], tmpb[:, u % 2, 0:w], h[:, cols].bitcast(F32),
                                  ALU.subtract).then_inc(hid_lo, 1)

            def up4(at, dyn, u, udyn, w, mlp, local, ldyn):
                for q in range(2):
                    split(at + 3 + 2 * q, dyn)
                    done(at + 2 * q + 1, dyn)
                    unit(u + q, udyn, w, mlp, local + q, ldyn,
                         between=lambda: split(at + 4 + 2 * q, dyn))
                    if mlp:
                        lower(u + q - 1, udyn, w, True, local + q - 1, ldyn)

            modf = mod[:].rearrange("p g k s -> p (g k s)")
            adabf = ada_b[:].rearrange("p g k s -> p (g k s)")

            def ada_mod(g, gdyn):
                dve.wait_ge(ada_cols_done, gdyn + (g + 1))
                cols = bass.ds(gdyn * 16 + g * 16, 16)
                parts = ps[:, 6, 0:32].rearrange("p (k h s) -> p k h s", h=2, s=2)
                out = modf[:, cols].rearrange("p (k s) -> p k s", s=2)
                dve.tensor_tensor(out, parts[:, :, 1, :], adabf[:, cols].rearrange("p (k s) -> p k s", s=2),
                                  ALU.add).then_inc(mod_begun, 1)
                dve.wait_ge(mod_begun, gdyn + (g + 1))
                dve.tensor_tensor(out, out, parts[:, :, 0, :], ALU.add).then_inc(mod_ready, 1)

            def ffn_up(name, w, ada_groups):
                at = START[name]
                local = 0
                if ada_groups:
                    with dve.Fori(0, ada_groups) as i:
                        for u in range(4):
                            for q in range(4):
                                split(at + 4 * u + q + 3, i * 16)
                            done(at + ADA_GROUP.index(("up", u)), i * 16)
                            unit(c["unit"] + u, i * 4, w, False, u, i * 4)
                        ada_mod(c["ada"], i)
                    at += 16 * ada_groups
                    c["unit"] += 4 * ada_groups
                    c["ada"] += ada_groups
                    local = 4 * ada_groups
                left = (START[name.replace("up", "down")] - at) // 4
                with dve.Fori(0, left) as i:
                    up4(at, i * 4, c["unit"], i * 2, w, False, local, i * 2)
                c["unit"] += 2 * left
                c["split"] = at + 4 * left + 3

            def mlp_up(name):
                at = START[name]
                split(at + 3)
                split(at + 4)
                input_inv()
                done(at + 1)
                dve.wait_ge(row_copied, c["cols"] - c["v"])
                unit(c["unit"], 0, S, True, 0, 0)
                split(at + 5)
                split(at + 6)
                done(at + 3)
                unit(c["unit"] + 1, 0, S, True, 1, 0)
                lower(c["unit"], 0, S, True, 0, 0)
                with dve.Fori(0, NM // 4 - 1) as i:
                    up4(at + 4, i * 4, c["unit"] + 2, i * 2, S, True, 2, i * 2)
                c["unit"] += NM // 2
                c["split"] = START[name] + NM + 3
                lower(c["unit"] - 1, 0, S, True, NM // 2 - 1, 0)

            def down(name, n_k):
                at = START[name]
                loops = n_k // 4 - 1
                with dve.Fori(0, loops) as i:
                    for q in range(4):
                        split(at + 3 + q, i * 4)
                c["split"] = at + 3 + 4 * loops
                split_to(at + n_k + 1)
                c["late"] = 1

            def short_down(name, n_k):
                split_to(START[name] + n_k + 1)
                c["late"] = 1

            def attention(l):
                units = attn_units(l)
                n = len(units)

                def normalise(u):
                    nk = len(units[u][5]) * P
                    dve.wait_ge(exp_ready, c["att"] + u + 1)
                    link(dve.reciprocal(srs[:, u:u + 1], ssm[:, u:u + 1]))
                    dve.tensor_scalar(prob[:, u % 4, 0:nk], prob[:, u % 4, 0:nk], srs[:, u:u + 1], None,
                                      ALU.mult).then_inc(prob_ready, 1)

                def o_lower(g):
                    _, s, t, *_ = units[4 * g]
                    part = slice(s * S, (s + 1) * S)
                    dve.wait_ge(o_hi, c["og"] + g + 1)
                    dve.tensor_tensor(nl[:, t, part], bank(4 + g % 2, S), nh[:, t, part].bitcast(F32),
                                      ALU.subtract).then_inc(o_lo, 1)

                for u, (g, s, t, h2, qt, kts) in enumerate(units):
                    nk = len(kts) * P
                    q = qcol(l, t, s, qt, h2)
                    dve.wait_ge(s_done, c["att"] + u + 1)
                    link(dve.tensor_reduce(smx[:, u:u + 1], ps[:, S_BANK[u % 4], 0:nk], AX.X, ALU.max))
                    dve.tensor_scalar(snm[:, u:u + 1], smx[:, u:u + 1], qscale[:, 1, q:q + 1], None,
                                      ALU.mult).then_inc(nmax_ready, 1)
                    if u:
                        normalise(u - 1)
                    if u >= 7 and u % 4 == 3:
                        o_lower(u // 4 - 1)
                normalise(n - 1)
                o_lower(n // 4 - 1)
                c["att"] += n
                c["og"] += n // 4

            def mixer1(l):
                w = mix_w(l)
                nq = 8 * (w // P)
                for i in range(IN_TILES):
                    split_to(in_slot(l, i) + 3)
                    if i == 3:
                        dve.wait_ge(hssq_done, 2 * l + 1)
                        link(dve.tensor_scalar(kqs[:, 0:T], bank(7), 1.0 / HD, EPS, ALU.mult, ALU.add))
                        dve.sem_inc(hms_read, 1)
                        dve.reciprocal(kqs[:, 0:T], kqs[:, 0:T]).then_inc(hrecip, 1)
                    if i == 6:
                        dve.wait_ge(hrstd, 2 * l + 1)
                        dve.tensor_tensor(kq[:, 0:T], kq[:, 0:T], kqs[:, 0:T], ALU.mult).then_inc(zn_ready, 1)
                    if i == 7:
                        dve.wait_ge(hssq_done, 2 * l + 2)
                        link(dve.tensor_scalar(qinv[:, 0, 0:nq], ps[:, 7, 0:nq], 1.0 / HD, EPS, ALU.mult, ALU.add))
                        dve.sem_inc(hms_read, 1)
                        dve.reciprocal(qinv[:, 1, 0:nq], qinv[:, 0, 0:nq]).then_inc(hrecip, 1)
                    if l == 0 and i == 6:
                        ada_mod(c["ada"], 0)
                        c["ada"] += 1
                    if i == 9:
                        dve.wait_ge(hrstd, 2 * l + 2)
                        link(dve.tensor_scalar(qscale[:, 1, 0:nq], qscale[:, 0, 0:nq], -1.0, None, ALU.mult))
                if l == 0:
                    ada_mod(c["ada"], 0)
                    c["ada"] += 1

                def rope(i, b):
                    a, _ = kq_at(i, w)
                    dve.wait_ge(rot_done, 5 * l + i + 1)
                    dve.tensor_tensor(rot[:, i % 2, :], bank(b, S), ccol("sin", 0, S), ALU.mult)
                    link(dve.tensor_tensor(kq[:, a:a + S], kq[:, a:a + S], ccol("cos", 0, S), ALU.mult))
                    dve.tensor_tensor(kq[:, a:a + S], kq[:, a:a + S], rot[:, i % 2, :], ALU.add).then_inc(qk_ready, 1)

                def channel(u):
                    dve.wait_ge(f1_done, c["f1"] + u + 1)
                    dve.tensor_copy(ab[:, u, :, :].rearrange("p a b -> p (a b)"), bank(u % 2)).then_inc(ab_ready, 1)

                dve.wait_ge(zn_ready, l + 1)
                rope(0, 4)
                rope(1, 5)
                channel(0)
                channel(1)
                rope(2, 4)
                rope(3, 5)
                for u in range(2, 2 * (w // S)):
                    channel(u)
                rope(4, 6)
                c["f1"] += 2 * (w // S)
                for s, part in enumerate(halves(w)):
                    for ch_ in range(2):
                        c["f2"] += 1
                        dve.wait_ge(f2_done, c["f2"])
                        dve.tensor_copy(yt[:, ch_, part], bank(2 + 2 * s + ch_, S)).then_inc(yt_ready, 1)
                for m in range(2):
                    dve.wait_ge(side_hi, 4 * l + m + 1)
                    dve.tensor_tensor(nl[:, 6 + m, 0:w], bank(6 + m, w), nh[:, 6 + m, 0:w].bitcast(F32),
                                      ALU.subtract).then_inc(side_lo, 1)
                for m in range(2):
                    dve.wait_ge(side_hi, 4 * l + m + 3)
                    dve.scalar_tensor_tensor(out=nl[:, 4 + m, 0:w], in0=bank(m, w),
                                             scalar=vcol("pool_scale", 2 * l + m),
                                             in1=nh[:, 4 + m, 0:w].bitcast(F32), op0=ALU.mult,
                                             op1=ALU.subtract).then_inc(side_lo, 1)
                attention(l)
                short_down(f"out{l}", KD)

            def softplus():
                e, d_, r_, z, z2 = (sp_t[:, k, :] for k in range(1, 6))
                lam = vec[:, VEC["lam"]:VEC["lam"] + 2 * NR]
                dve.wait_ge(sp_step, 1)
                link(dve.tensor_scalar(d_, e, 2.0, None, ALU.add))
                link(dve.reciprocal(r_, d_))
                link(dve.tensor_tensor(z, e, r_, ALU.mult))
                link(dve.tensor_tensor(z2, z, z, ALU.mult))
                link(dve.tensor_scalar(d_, z2, 1.0 / 17, None, ALU.mult))
                for k in (15, 13, 11, 9, 7, 5, 3):
                    link(dve.scalar_tensor_tensor(out=d_, in0=d_, scalar=1.0 / k, in1=z2, op0=ALU.add, op1=ALU.mult))
                link(dve.scalar_tensor_tensor(out=d_, in0=d_, scalar=1.0, in1=z, op0=ALU.add, op1=ALU.mult))
                link(dve.tensor_scalar(r_, lam, -1.0, 0.0, ALU.mult, ALU.max))
                link(dve.scalar_tensor_tensor(out=d_, in0=d_, scalar=2.0, in1=r_, op0=ALU.mult, op1=ALU.add))
                dve.tensor_scalar(n4sp[:], d_, -4.0, None, ALU.mult).then_inc(sp_step, 1)

            dve.sem_inc(up_evac, 2)
            dve.sem_inc(hid_lo, 2)
            dve.wait_ge(c_hi_ready, 1)
            view = cst4[:, 0:32].rearrange("p (k c) -> p k c", c=4)
            dve.tensor_tensor(view[:, :, 2:4], csil[:], view[:, :, 0:2].bitcast(F32),
                              ALU.subtract).then_inc(c_ready, 1)
            for g in range(2):
                split_to(10)
                if g:
                    dve.wait_ge(x_loaded, 16)
                    dve.sem_inc(x_new, KD)
                    split_to(16)
                    add_last(T)
                    split_to(17)
                    inv_of_sums(T)
                    split_to(18)
                ada_mod(g, 0)
                c["ada"] += 1
            for l in range(DEPTH):
                fix_one(l, 0, 1)
                norm_mod(T, l, MOD(l, 0), 5 * l, begun=(l == 0))
                ffn_up(f"ffn1_up{l}", T, 5 if l == 0 else 4)
                if l == 0:
                    softplus()
                down(f"ffn1_down{l}", NF)
                fix_one(l, 3, 2)
                fix_one(l, 1, 4)
                residual(f"ffn1_down{l}", T, fix[:, 5 * l + 3, :, :])
                norm_mod(T, l, MOD(l, 3), 5 * l + 1)
                mixer1(l)
                w = mix_w(l)
                fix_one(l, 2, 7)
                fix_one(l, 4, 8)
                dve.wait_ge(mod_ready, MOD(l, 5) + 1)
                residual(f"out{l}", w, mod[:, MOD(l, 5), :, :])
                norm_mod(w, l, MOD(l, 6), 5 * l + 2)
                ffn_up(f"ffn2_up{l}", w, 5 if l == 0 else 0)
                down(f"ffn2_down{l}", NF)
                residual(f"ffn2_down{l}", w, fix[:, 5 * l + 4, :, :])
            c["ffn_units"] = c["unit"]
            norm_last("final1", lambda m: ("norm_mix", m))

            def b_lower(h, l_, m):
                dve.wait_ge(b_hi, c["b"] + m + 1)
                dve.tensor_tensor(l_[:, m, :], tmpb[:, m % 2, 0:S], h[:, m, :].bitcast(F32),
                                  ALU.subtract).then_inc(b_lo, 1)

            def evac(dst, n, at):
                done(at + n)
                dve.tensor_tensor(dst, bank(n % 4, S), rstd_row[:], ALU.mult).then_inc(b_evac, 1)

            def rglru(i, j):
                at = START[f"b_in{i}"]
                split_to(at + 4)
                input_inv()
                split_to(at + 5)
                dve.wait_ge(row_copied, c["cols"] - c["v"])
                dve.wait_ge(pads_ready, DEPTH + (1 if i == 0 else 3))

                def gate_part(n):
                    g = n if n < HEAD_G else n - NR
                    split_to(at + n + 3)
                    evac(gelu_g[:, g, :], n, at)

                def decay(m):
                    dve.wait_ge(th_ready, c["cv"] + m + 1)
                    link(dve.tensor_scalar(av[:, m, :], th[:, m, :], -1.0, 1.0, ALU.mult, ALU.add))
                    if m >= 3:
                        dve.wait_ge(ix_ready, 3 * c["cv"] + 2 * (m - 2))
                    link(dve.reciprocal(dd[:, m % 3, :], av[:, m, :]))
                    dve.scalar_tensor_tensor(out=av[:, m, :], in0=th[:, m, :], scalar=1.0, in1=dd[:, m % 3, :],
                                             op0=ALU.add, op1=ALU.mult).then_inc(av_ready, 1)

                for n in range(HEAD_G):
                    gate_part(n)
                for m in range(NR):
                    split_to(at + HEAD_G + m + 3)
                    if m >= 2:
                        dve.wait_ge(cv_ready, c["cv"] + m - 1)
                    evac(xpad[:, m % 2, 3:3 + S], HEAD_G + m, at)
                    if m >= 3:
                        decay(m - 3)
                    dve.wait_ge(cv_begun, c["cv"] + m + 1)
                    for tap in range(3):
                        ins = dve.scalar_tensor_tensor(
                            out=cv[:, m, :], in0=xpad[:, m % 2, tap:tap + S],
                            scalar=vcol("conv_w", (j * 4 + tap) * NR + m), in1=cv[:, m, :],
                            op0=ALU.mult, op1=ALU.add)
                        if tap < 2:
                            link(ins)
                    ins.then_inc(cv_ready, 1)
                tail = HEAD_G + NR

                def product(m):
                    dve.wait_ge(ix_ready, 3 * c["cv"] + 2 * NR + m + 1)
                    link(dve.tensor_tensor_scan(hs[:, m % 2, :], av[:, m, :], ix[:, m, :], 0.0, ALU.mult, ALU.add))
                    if m >= 2:
                        dve.wait_ge(b_lo, c["b"] + m - 1)
                    dve.wait_ge(gelu_ready, c["gelu"] + m + 1)
                    dve.tensor_tensor(tmpb[:, m % 2, 0:S], hs[:, m % 2, :], gelu_g[:, m, :],
                                      ALU.mult).then_inc(b_f32, 1)
                    if m:
                        b_lower(oh, ol, m - 1)

                gate_part(tail)
                decay(NR - 3)
                gate_part(tail + 1)
                decay(NR - 2)
                decay(NR - 1)
                split_to(at + tail + 5)
                for n in range(tail + 2, 2 * NR):
                    evac(gelu_g[:, n - NR, :], n, at)
                    for m in RNN_TAIL[n - tail]:
                        product(m)
                    split_to(at + n + 4)
                for m in range(RNN_TAIL[-1][-1] + 1, NR):
                    product(m)
                    split_to(START[f"b_out{i}"] + m - 1)
                b_lower(oh, ol, NR - 1)
                c["cv"] += NR
                c["b"] += NR
                c["bev"] += 2 * NR
                c["gelu"] += NR
                short_down(f"b_out{i}", NR)

            def sgu(i):
                at = START[f"b_in{i}"]
                split_to(at + 4)
                input_inv()
                split_to(at + 5)
                dve.wait_ge(row_copied, c["cols"])
                for m in range(2 * KD):
                    split_to(at + m + 3)
                    if m >= 2:
                        dve.wait_ge(gelu_ready, c["gelu"] + m - 1)
                    evac(zrow[:, m % 2, :], m, at)
                    if m == KD:
                        c["v"] = 1
                        c["cols"] += 1
                        dve.wait_ge(col_sums, c["cols"])
                        mean_square(4, S)
                    if m >= KD:
                        for k in SGU_GATED[m - KD]:
                            gated(k)
                c["b"] += KD
                c["bev"] += 2 * KD
                c["gelu"] += 2 * KD
                short_down(f"b_out{i}", KD)

            def gated(m):
                dve.wait_ge(mixd_done, m + 1)
                dve.wait_ge(gelu_ready, c["gelu"] + KD + m + 1)
                if m >= 2:
                    dve.wait_ge(b_lo, c["b"] + m - 1)
                dve.tensor_tensor(tmpb[:, m % 2, 0:S], bank(6 + m % 2, S), ug[:, m, :], ALU.mult).then_inc(b_f32, 1)
                b_lower(oh, ol, m)

            def conv(i):
                at = START[f"b_in{i}"]
                split_to(at + 4)
                input_inv()
                split_to(at + 5)
                dve.wait_ge(row_copied, c["cols"] - c["v"])
                dve.wait_ge(pads_ready, DEPTH + 2)
                for m in range(KD):
                    split_to(at + 3 * m + 4)
                    acc = tmpb[:, m % 2, 0:S]
                    gc = gcr[:, m % 2, :]
                    b = 3 * (m % 2)
                    done(at + 3 * m + 1)
                    link(dve.tensor_tensor(gc, bank(b, S), inv_row[:, 0:S], ALU.mult))
                    link(dve.tensor_tensor(cpad[:, m % 2, 2:2 + S], gc, bank(b + 1, S), ALU.mult))
                    link(dve.tensor_scalar(acc, cpad[:, m % 2, 0:S], vcol("c_conv", m), None, ALU.mult))
                    for tap in (1, 2):
                        link(dve.scalar_tensor_tensor(out=acc, in0=cpad[:, m % 2, tap:tap + S],
                                                      scalar=vcol("c_conv", tap * KD + m), in1=acc,
                                                      op0=ALU.mult, op1=ALU.add))
                    link(dve.tensor_tensor(acc, acc, rstd_row[:], ALU.mult))
                    done(at + 3 * m + 2)
                    dve.tensor_tensor(acc, acc, bank(b + 2, S), ALU.mult).then_inc(b_f32, 1)
                    split_to(at + 3 * m + 6)
                    b_lower(oh, ol, m)
                c["b"] += KD
                short_down(f"b_out{i}", KD)

            for i, kind in enumerate(MIXERS):
                if kind == "rglru":
                    rglru(i, i // 3)
                elif kind == "sgu":
                    sgu(i)
                else:
                    conv(i)
                residual(f"b_out{i}", S, None, lambda m, i=i: ("norm_mlp", i * KD + m))
                mlp_up(f"mlp_up{i}")
                down(f"mlp_down{i}", NM)
                residual(f"mlp_down{i}", S, None,
                         (lambda m, i=i: ("norm_mix", (i + 1) * KD + m)) if i + 1 < len(MIXERS) else None)
            norm_last("final2")

        @block.gpsimd
        def _(pool):
            c = Tally()

            def link(ins):
                c["chain"] += 1
                ins.then_inc(pool_chain, 1)
                pool.wait_ge(pool_chain, c["chain"])

            def norm_squares(w, before=0):
                c["norm"] += 1
                base = (c["norm"] - 1) * KD + before
                for m in range(1, KD - 2):
                    pool.wait_ge(sq_ready, base + m + 1)
                    if m == 1:
                        if c["norm"] > 1:
                            pool.wait_ge(sq_summed, c["norm"] - 1)
                        first = norm_buf(0)[:, 0:w]
                    else:
                        pool.wait_ge(part_added, c["part"])
                        first = sqsum[:, 0:w]
                    pool.tensor_tensor(sqsum[:, 0:w], first, norm_buf(m)[:, 0:w], ALU.add).then_inc(part_added, 1)
                    c["part"] += 1

            pool.memset(ones[:], 1.0)
            pool.memset(cst4[:].bitcast(F32), 0.0).then_inc(consts_ready, 1)
            for l in range(DEPTH):
                w = mix_w(l)
                seg = w // S
                norm_squares(T)
                norm_squares(T)
                pool.wait_ge(slots_done, RING + START[f"in{l}"])
                pool.dma_start(cst[:], cst_in).then_inc(mix_loaded, 16)
                pool.dma_start(fftw[:], fftw_in[l]).then_inc(mix_loaded, 16)
                pool.dma_start(poolw[:], poolw_in[l]).then_inc(mix_loaded, 16)
                pool.memset(up[:], 0.0).then_inc(pads_ready, 1)
                pool.wait_ge(z_ready, 10 * l + 8)
                u = up[:, :, 0:seg, :]
                link(pool.tensor_tensor(w2[:, :, 0:seg, 1:PADW], u[:, :, :, 0:PADW - 1], u[:, :, :, 1:PADW],
                                        ALU.add))
                link(pool.tensor_tensor(w4[:, :, 0:seg, 2:PADW - 1], w2[:, :, 0:seg, 1:PADW - 2],
                                        w2[:, :, 0:seg, 3:PADW], ALU.add))
                link(pool.tensor_tensor(w8[:, 0:seg, 4:PADW - 3], w4[:, 1, 0:seg, 2:PADW - 5],
                                        w4[:, 1, 0:seg, 6:PADW - 1], ALU.add))
                link(pool.tensor_tensor(w16[:, 0:seg, 8:8 + S], w8[:, 0:seg, 4:4 + S], w8[:, 0:seg, 12:12 + S],
                                        ALU.add))
                pool.wait_ge(mix_loaded, 48 * (l + 1))
                cnt = cst[:, CST["inv_cnt"]:CST["inv_cnt"] + 2 * S].rearrange("p (a t) -> p a t", a=2)
                lo, hi = slice(0, 64), slice(64, 128)
                for s in range(seg):
                    for rows, tile, sums in ((lo, 0, w2[lo, 0, s, 8:8 + S]), (hi, 0, w4[hi, 0, s, 8:8 + S]),
                                             (lo, 1, w8[lo, s, 8:8 + S]), (hi, 1, w16[hi, s, 8:8 + S])):
                        last = pool.tensor_tensor(pc[rows, tile, s, :], sums, cnt[rows, tile, :], ALU.mult)
                link(last)
                pool.tensor_tensor(pc[:, :, 0:seg, :], pc[:, :, 0:seg, :], up[:, :, 0:seg, 8:8 + S],
                                   ALU.subtract).then_inc(pool_ready, 1)
                norm_squares(w)

            def load_gates(j, ready):
                pool.wait_ge(x_new, ready * KD)
                pool.dma_start(gates_w[:], gate_in[j]).then_inc(gates_loaded, 16)

            load_gates(0, 3 * DEPTH)
            norm_squares(S)

            def add_squares(src, ready, base, added, first_free, also=None):
                for m in range(KD):
                    pool.wait_ge(ready, base + m + 1)
                    if m == 0:
                        if first_free:
                            pool.wait_ge(col_sums, first_free)
                        pool.tensor_copy(sqsum[:, 0:S], src(m)).then_inc(added, 1)
                    else:
                        pool.wait_ge(added, c[added.name] + m)
                        pool.tensor_tensor(sqsum[:, 0:S], sqsum[:, 0:S], src(m), ALU.add).then_inc(added, 1)
                    if also:
                        also(m)
                c[added.name] += KD

            def input_squares():
                add_squares(square_buf, sq_ready, NORM_SQ + c["sb"], sq_added, c["cols"])
                c["sb"] += KD
                c["cols"] += 1

            for i, kind in enumerate(MIXERS):
                input_squares()
                pool.wait_ge(x_new, (2 + 3 * DEPTH + 2 * i) * KD)
                if kind == "rglru":
                    pool.memset(xpad[:, :, 0:3], 0.0).then_inc(pads_ready, 1)
                    for m in range(NR):
                        pool.wait_ge(gate_ready, c["cv"] + m + 1)
                        pool.wait_ge(cv_ready, c["cv"] + m + 1)
                        pool.tensor_tensor(ix[:, m, :], sg[:, m % 2, S:T], cv[:, m, :], ALU.mult
                                           ).then_inc(ix_ready, 1)
                        pool.wait_ge(ix_ready, 3 * c["cv"] + 2 * m + 1)
                        pool.wait_ge(av_ready, c["cv"] + m + 1)
                        pool.tensor_tensor(ix[:, m, :], ix[:, m, :], dd[:, m % 3, :], ALU.mult
                                           ).then_inc(ix_ready, 1)
                    for m in range(NR):
                        if m % 5 == 0:
                            c["root_b"] += 1
                            pool.wait_ge(root_ready, c["root_b"])
                            pool.wait_ge(ix_ready, 3 * c["cv"] + 2 * NR)
                        pool.tensor_tensor(ix[:, m, :], ix[:, m, :], th[:, m, :], ALU.mult).then_inc(ix_ready, 1)
                    c["cv"] += NR
                elif kind == "sgu":
                    pool.dma_start(sbias[:], sb_in).then_inc(small_loaded, 16)
                    pool.dma_start(ws[:], ws_in).then_inc(small_loaded, 16)
                    pool.wait_ge(small_loaded, 32)
                    pool.affine_select(out=ws[:], in_=ws[:], compare_op=ALU.is_ge, fill=0.0, base=0,
                                       pattern=[[0, KD], [1, P]], channel_multiplier=-1).then_inc(ws_ready, 1)
                    def scale(m):
                        pool.tensor_scalar(vg[:, m, :], vg[:, m, :], vcol("b_norm", m), None, ALU.mult
                                           ).then_inc(vg_scaled, 1)

                    add_squares(lambda m: vsq[:, m % 2, :], vsq_ready, 0, v_added, c["cols"], also=scale)
                    c["cols"] += 1
                else:
                    pool.memset(cpad[:, :, 0:2], 0.0).then_inc(pads_ready, 1)
                input_squares()
                if i + 1 < len(MIXERS) and i and MIXERS[i + 1] == "rglru":
                    load_gates(1, 3 + 3 * DEPTH + 2 * i)
            pool.wait_ge(col_sums, c["cols"])
            norm_squares(S, 2 * len(MIXERS) * KD)


def MOD(l, g):
    return ADA_ORDER.index((l, g))


def up_slots(w, kd=KD):
    m = w.shape[1] // P
    return w.reshape(kd, P, m, P).transpose(2, 1, 0, 3).reshape(m, P, kd * P)


def down_slots(w):
    return w.reshape(w.shape[0] // P, P, SLOT)


def ada_slots(w, g):
    return w[:, g * SLOT:(g + 1) * SLOT].reshape(KD, P, SLOT)


def columns(v):
    return v.reshape(-1, P).T


def tables():
    f4 = np.float32
    t = np.arange(S)
    inv = (f4(10000.0) ** (-np.arange(HD // 4, dtype=f4) / f4(HD // 4))).astype(f4)
    row, col = (t // GRID_W).astype(f4), (t % GRID_W).astype(f4)
    ang = np.concatenate([row[:, None] * inv, col[:, None] * inv], axis=-1).astype(f4)
    which = np.arange(P) % (HD // 2)
    cst = np.zeros((P, N_CST), f4)

    def put(name, a):
        cst[:, CST[name]:CST[name] + a.shape[1]] = a

    put("cos", np.cos(ang).T[which])
    put("sin", np.sin(ang).T[which])
    ch = np.arange(HD)
    wc = 2 * np.pi * np.outer(ch, ch) / HD
    eye = np.eye(2)
    put("dft_c", np.concatenate([np.kron(eye, np.cos(wc)), np.kron(eye, np.sin(wc))], axis=1))
    wt = 2 * np.pi * (np.outer(t, t) % S) / S
    norm = 1.0 / np.sqrt(S * HD)
    cs = np.stack([np.cos(wt), -np.sin(wt)]) * norm
    put("dft_s", cs.reshape(2, 2, P, S).transpose(2, 1, 0, 3).reshape(P, 4 * S))
    cnt = np.zeros((2, P, S))
    for g, w in enumerate((2, 4, 8, 16)):
        n = np.clip(t + w - w // 2, 0, S) - np.clip(t - w // 2, 0, S)
        cnt[g // 2, 64 * (g % 2):64 * (g % 2) + 64] = 1.0 / n
    put("inv_cnt", cnt.transpose(1, 0, 2).reshape(P, 2 * S))
    swap = np.zeros((P, P))
    for m in range(P):
        if m % HD < HD // 2:
            swap[m + HD // 2, m] = -1.0
        else:
            swap[m - HD // 2, m] = 1.0
    put("swap", swap)
    put("blk", np.kron(eye, np.ones((HD, HD))))
    return cst


def kernel(**inputs):
    import concourse.bacc as bacc
    from concourse.bass_utils import run_bass_kernel_spmd

    v = {k: np.asarray(a) for k, a in inputs.items()}
    stream = np.empty((N_SLOTS, P, SLOT), np.float32)

    def put(name, a, skip=0):
        stream[START[name] + skip:START[name] + skip + len(a)] = a

    heads = [h for t in range(4) for h in (t, t + 4)]
    order = np.concatenate([np.arange(h * HD, (h + 1) * HD) for h in heads])
    aw = 8 * HD
    in_cols = np.concatenate([np.arange(aw, aw + 2 * P), order, np.arange(aw + 2 * P, aw + 6 * P)])

    def ffn_up(name, w, groups):
        half = w.shape[1] // 2
        g, u = up_slots(w[:, :half]), up_slots(w[:, half:])
        slots = np.stack([g, u], axis=1).reshape(2 * NF, P, SLOT)
        at = 0
        for n, (l, grp) in enumerate(groups):
            a = ada_slots(v["ada_w"][l], grp)
            for k, (what, q) in enumerate(ADA_GROUP):
                one = a[q] if what == "ada" else slots[8 * n + 2 * q + (what == "up")]
                put(name, one[None], 16 * n + k)
            at = 8 * (n + 1)
        put(name, slots[at:], 16 * len(groups))

    put("ada_head", np.concatenate([ada_slots(v["ada_w"][0], g) for g in (0, 1)]))
    for l in range(DEPTH):
        ffn_up(f"ffn1_up{l}", v["ffn1_w_gu"][l], ADA_ORDER[2:7] if l == 0 else ADA_ORDER[14:18])
        put(f"ffn1_down{l}", down_slots(v["ffn1_w_down"][l]))
        tiles = up_slots(v["w_in"][l][:, in_cols])
        if l == 0:
            a = np.concatenate([ada_slots(v["ada_w"][0], g) for g in (7, 8)]).reshape(KD, 2, P, SLOT)
            middle = np.concatenate([tiles[1:KD + 1, None], a], axis=1).reshape(3 * KD, P, SLOT)
            tiles = np.concatenate([tiles[:1], middle, tiles[KD + 1:]])
        put(f"in{l}", tiles)
        w = v["w_out"][l]
        w = down_slots(np.concatenate([w[order], w[aw:]]))
        put(f"out{l}", w[[4, 5, 6, 7, 0, 1, 2, 3]])
        ffn_up(f"ffn2_up{l}", v["ffn2_w_gu"][l], ADA_ORDER[9:14] if l == 0 else [])
        put(f"ffn2_down{l}", down_slots(v["ffn2_w_down"][l]))
    for i, kind in enumerate(MIXERS):
        if kind == "rglru":
            w = up_slots(v["a_w_in_2"][i // 3])
            put(f"b_in{i}", np.concatenate([w[:HEAD_G], w[NR:], w[HEAD_G:NR]]))
            put(f"b_out{i}", down_slots(v["a_w_out_2"][i // 3]))
        elif kind == "sgu":
            w = up_slots(v["b_w_in_2"][0])
            put(f"b_in{i}", np.concatenate([w[KD:], w[:KD]]))
            put(f"b_out{i}", down_slots(v["b_w_out_2"][0]))
        else:
            w = up_slots(v["c_w_in_2"][0]).reshape(3, KD, P, SLOT)
            put(f"b_in{i}", w[[1, 2, 0]].transpose(1, 0, 2, 3).reshape(3 * KD, P, SLOT))
            put(f"b_out{i}", down_slots(v["c_w_out_2"][0]))
        put(f"mlp_up{i}", up_slots(v["mlp_w1_2"][i]))
        put(f"mlp_down{i}", down_slots(v["mlp_w2_2"][i]))

    vec = np.zeros((P, N_VEC), np.float32)

    def vput(name, a):
        vec[:, VEC[name]:VEC[name] + a.shape[1]] = a

    for name, key in [("final1", "final_gain"), ("final2", "final_norm_g_2"), ("norm_mix", "norm_mix_g_2"),
                      ("norm_mlp", "norm_mlp_g_2"), ("conv_w", "a_conv_w_2"), ("conv_b", "a_conv_b_2"),
                      ("ba", "a_gate_a_b_2"), ("bx", "a_gate_x_b_2"), ("lam", "a_lambda_2"),
                      ("b_norm", "b_norm_g_2"), ("c_conv", "c_conv_w_2"), ("pool_scale", "pool_scale")]:
        vput(name, columns(v[key]))
    vput("q_gain", np.concatenate([v["q_gain"], v["q_gain"]], axis=1).T)
    vput("k_gain", np.concatenate([v["k_gain"], v["k_gain"]], axis=1).T)

    ada_b = np.stack([v["ada_b"][l, g * D:(g + 1) * D].reshape(KD, P).T for l, g in ADA_ORDER], axis=1)
    poolw = np.zeros((DEPTH, P, 2, P), np.float32)
    for g in range(4):
        o = 64 * (g % 2)
        poolw[:, o:o + 64, g // 2, o:o + 64] = v["pool_w"][:, g]
    gates = np.zeros((2, P, 2, len(GATE_BLOCKS), P), np.float32)
    for g, key in enumerate(("a_gate_a_w_2", "a_gate_x_w_2")):
        full = np.zeros((2, D_RNN, D_RNN), np.float32)
        for h in range(D_RNN // A_HD):
            rows = slice(h * A_HD, (h + 1) * A_HD)
            full[:, rows, rows] = v[key][:, h]
        for n, (k, m) in enumerate(GATE_BLOCKS):
            gates[:, :, g, n] = full[:, k * P:(k + 1) * P, m * P:(m + 1) * P]
    x = np.zeros((P, KD, T), np.float32)
    x[:, :, :S] = v["x"][0].T.reshape(KD, P, S).transpose(1, 0, 2)
    x[:, :, S:] = v["ctx"][0].T.reshape(KD, P, S).transpose(1, 0, 2)
    cst = tables()
    arrays = {
        "x_in": x,
        "stream": stream,
        "vec_in": vec,
        "cvec_in": np.stack([v["c"][0].reshape(KD, P).T, v["c_ctx"].reshape(KD, P).T], axis=2),
        "ada_b_in": np.stack([ada_b, ada_b], axis=3),
        "cst_in": cst,
        "ident_in": np.eye(P, dtype=np.float32),
        "fftw_in": v["fft_w"].reshape(DEPTH, 2, P, 2 * P).transpose(0, 2, 1, 3),
        "poolw_in": poolw,
        "gate_in": gates,
        "ws_in": v["b_w_s_2"][0].transpose(2, 0, 1),
        "sb_in": v["b_s_bias_2"][0].reshape(1, KD * P),
    }
    nc = bacc.Bacc("TRN2", target_bir_lowering=False, num_devices=1)
    arrays = {k: np.ascontiguousarray(a) for k, a in arrays.items()}
    args = [nc.dram_tensor(k, a.shape, mybir.dt.from_np(a.dtype), kind="ExternalInput").ap()
            for k, a in arrays.items()]
    out = nc.dram_tensor("out", (P, KD, S), F32, kind="ExternalOutput").ap()
    build(nc, *args, out)
    r = run_bass_kernel_spmd(nc, [arrays], core_ids=[0])
    got = np.asarray(r.results[0]["out"])
    return np.ascontiguousarray(got.transpose(2, 1, 0).reshape(1, S, D))
```
